# Optimizing a Trainium2 kernel written in Bass

```python
import jax, jax.numpy as jnp
from jax import lax
import numpy as np

D_MODEL = 2048
BATCH = 1
SEQ = 512
DEPTH = 1

GRID_W = 64
PLE_DIM = 256
HG_HEADS = 8
HG_DK = 128
HG_DV = 128
HG_W = HG_HEADS * HG_DK
HG_CHUNK = 64
NA_HEADS = 8
NA_HD = 128
NA_W = NA_HEADS * NA_HD
NA_KH = 8
NA_KW = 16
N_IN = 5 * HG_W + 4 * NA_W + 2 * D_MODEL
EPS = 1e-6
NEG = -1e30
F_MIN = 1e-6

kernel_name = "hybrid_hgrn2_natten_gated_encoder"

_SPLITS = [HG_W, 2 * HG_W, 3 * HG_W, 4 * HG_W, 5 * HG_W,
           5 * HG_W + NA_W, 5 * HG_W + 2 * NA_W, 5 * HG_W + 3 * NA_W,
           5 * HG_W + 4 * NA_W, 5 * HG_W + 4 * NA_W + D_MODEL]

def _rms(x, g):
    xf = x.astype(jnp.float32)
    y = xf * lax.rsqrt(jnp.mean(xf * xf, axis=-1, keepdims=True) + EPS)
    return (y * g.astype(jnp.float32)).astype(x.dtype)

def _gla_scan(q, k, v, logf):
    B, S, H, dk = q.shape
    C = HG_CHUNK
    n = S // C

    def to_chunks(a):
        return a.astype(jnp.float32).reshape(B, n, C, H, a.shape[-1]).transpose(1, 0, 3, 2, 4)

    qc, kc, vc, gc = to_chunks(q), to_chunks(k), to_chunks(v), to_chunks(logf)
    tri = jnp.tril(jnp.ones((C, C), dtype=bool))

    def step(state, xs):
        qb, kb, vb, gb = xs
        b = jnp.cumsum(gb, axis=-2)
        o_inter = jnp.einsum('bhtk,bhkv->bhtv', qb * jnp.exp(b), state)
        diff = b[:, :, :, None, :] - b[:, :, None, :, :]
        decay = jnp.exp(jnp.where(tri[:, :, None], diff, NEG))
        att = jnp.einsum('bhtk,bhsk,bhtsk->bhts', qb, kb, decay)
        o_intra = jnp.einsum('bhts,bhsv->bhtv', att, vb)
        b_last = b[:, :, -1:, :]
        new_state = state * jnp.exp(b_last[:, :, 0, :, None]) + jnp.einsum(
            'bhsk,bhsv->bhkv', kb * jnp.exp(b_last - b), vb)
        return new_state, o_inter + o_intra

    s0 = jnp.zeros((B, H, dk, v.shape[-1]), jnp.float32)
    _, out = lax.scan(step, s0, (qc, kc, vc, gc))
    return out.transpose(1, 0, 3, 2, 4).reshape(B, S, H, v.shape[-1])

def _hgrn2_bidir(q_raw, i_raw, z_fwd, z_bwd, lb_fwd, lb_bwd):
    B, S, _ = q_raw.shape
    q = jax.nn.silu(q_raw).reshape(B, S, HG_HEADS, HG_DK)
    v = i_raw.reshape(B, S, HG_HEADS, HG_DV)

    def gates(z, lb):
        z = z.astype(jnp.float32).reshape(B, S, HG_HEADS, HG_DK)
        lb = lb.reshape(HG_HEADS, HG_DK)
        f = lb + (1.0 - lb) * jax.nn.sigmoid(z)
        logf = jnp.log(jnp.maximum(f, F_MIN))
        k = (1.0 - lb) * jax.nn.sigmoid(-z)
        return k, logf

    kf, gf = gates(z_fwd, lb_fwd)
    kb, gb = gates(z_bwd, lb_bwd)
    o_f = _gla_scan(q, kf, v, gf)
    rev = lambda a: jnp.flip(a, axis=1)
    o_b = rev(_gla_scan(rev(q), rev(kb), rev(v), rev(gb)))
    return o_f + o_b

def _neighbourhood_attention(q, k, v, rpb):
    B, S, H, hd = q.shape
    rows = S // GRID_W
    kh = min(NA_KH, rows)
    kw = NA_KW
    r = jnp.arange(rows)
    r_start = jnp.clip(r - kh // 2, 0, rows - kh)
    ridx = r_start[:, None] + jnp.arange(kh)[None, :]
    c = jnp.arange(GRID_W)
    c_start = jnp.clip(c - kw // 2, 0, GRID_W - kw)
    col_in = (c[None, :] >= c_start[:, None]) & (c[None, :] < c_start[:, None] + kw)

    qg = q.reshape(B, rows, GRID_W, H, hd)
    kg = k.reshape(B, rows, GRID_W, H, hd)[:, ridx]
    vg = v.reshape(B, rows, GRID_W, H, hd)[:, ridx]

    s = jnp.einsum('brqhd,brakhd->brhqak', qg, kg).astype(jnp.float32) * (hd ** -0.5)
    row_off = ridx - r[:, None] + (NA_KH - 1)
    col_off = jnp.clip(c[None, :] - c[:, None] + (NA_KW - 1), 0, 2 * NA_KW - 2)
    bias = rpb.astype(jnp.float32)[:, row_off[:, None, :, None], col_off[None, :, None, :]]
    bias = bias.transpose(1, 0, 2, 3, 4)
    s = jnp.where(col_in[None, None, None, :, None, :], s + bias[None], NEG)
    pr = jax.nn.softmax(s.reshape(B, rows, H, GRID_W, kh * GRID_W), axis=-1).reshape(s.shape)
    o = jnp.einsum('brhqak,brakhd->brqhd', pr.astype(v.dtype), vg)
    return o.reshape(B, S, H * hd)

def setup_inputs(seed: int = 0) -> dict:
    key = jax.random.key(seed)
    ks = jax.random.split(key, 16)
    n = jax.random.normal
    f32 = jnp.float32
    return {
        "x": n(ks[0], (BATCH, SEQ, D_MODEL), f32),
        "p": n(ks[1], (DEPTH, BATCH, SEQ, PLE_DIM), f32),
        "norm_g": 1.0 + 0.02 * n(ks[2], (DEPTH, D_MODEL), f32),
        "w_in": n(ks[3], (DEPTH, D_MODEL, N_IN), f32) * D_MODEL ** -0.5,
        "hgrn_lb": n(ks[4], (DEPTH, 2, HG_W), f32),
        "hgrn_onorm": 1.0 + 0.02 * n(ks[5], (DEPTH, HG_DV), f32),
        "na_qnorm": 1.0 + 0.02 * n(ks[6], (DEPTH, NA_HD), f32),
        "na_knorm": 1.0 + 0.02 * n(ks[7], (DEPTH, NA_HD), f32),
        "na_rpb": 0.02 * n(ks[8], (DEPTH, NA_HEADS, 2 * NA_KH - 1, 2 * NA_KW - 1), f32),
        "w_branch_a": n(ks[9], (DEPTH, HG_W, D_MODEL), f32) * HG_W ** -0.5,
        "w_branch_b": n(ks[10], (DEPTH, NA_W, D_MODEL), f32) * NA_W ** -0.5,
        "w_out": n(ks[11], (DEPTH, D_MODEL, D_MODEL), f32) * D_MODEL ** -0.5,
        "ple_norm": 1.0 + 0.02 * n(ks[12], (DEPTH, D_MODEL), f32),
        "w_ple_gate": n(ks[13], (DEPTH, D_MODEL, D_MODEL), f32) * D_MODEL ** -0.5,
        "w_ple": n(ks[14], (DEPTH, PLE_DIM, D_MODEL), f32) * PLE_DIM ** -0.5,
    }

def reference(x, p, norm_g, w_in, hgrn_lb, hgrn_onorm, na_qnorm, na_knorm, na_rpb,
              w_branch_a, w_branch_b, w_out, ple_norm, w_ple_gate, w_ple):
    B, S, _ = x.shape
    lbp = jax.nn.softmax(hgrn_lb.astype(jnp.float32), axis=0)
    lower = jnp.cumsum(lbp, axis=0) - lbp[0:1]

    for i in range(DEPTH):
        h = _rms(x, norm_g[i])
        u = h @ w_in[i]
        (hq, hi, hf_fwd, hf_bwd, hgate, nq, nk, nv, ngate, m_a, m_b) = jnp.split(u, _SPLITS, axis=-1)

        oa = _hgrn2_bidir(hq, hi, hf_fwd, hf_bwd, lower[i, 0], lower[i, 1])
        oa = _rms(oa, hgrn_onorm[i]).reshape(B, S, HG_W).astype(x.dtype)
        ya = (oa * jax.nn.silu(hgate)) @ w_branch_a[i]

        q = _rms(nq.reshape(B, S, NA_HEADS, NA_HD), na_qnorm[i])
        k = _rms(nk.reshape(B, S, NA_HEADS, NA_HD), na_knorm[i])
        v = nv.reshape(B, S, NA_HEADS, NA_HD)
        ob = _neighbourhood_attention(q, k, v, na_rpb[i])
        yb = (ob * jax.nn.silu(ngate)) @ w_branch_b[i]

        y = jax.nn.sigmoid(m_a) * ya + jax.nn.sigmoid(m_b) * yb
        x = x + y @ w_out[i]

        g = jax.nn.sigmoid(_rms(x, ple_norm[i]) @ w_ple_gate[i])
        x = x + (p[i] @ w_ple[i]) * g
    return x


_drawn_inputs = setup_inputs


def setup_inputs(seed=0):
    import zlib

    import numpy as np

    out = dict(_drawn_inputs(seed))
    spreads = {}
    factors = {'norm_g': 6.518,
     'hgrn_onorm': 24.705,
     'na_qnorm': 8.0,
     'na_knorm': 8.0,
     'na_rpb': 100.382,
     'ple_norm': 200.0,
     'w_ple_gate': 31.584,
     'p': 6.245,
     'w_ple': 6.248}
    for name, (base, spread) in spreads.items():
        noise = np.random.default_rng([zlib.crc32(name.encode()), seed]).standard_normal(out[name].shape)
        drawn = base * np.exp(spread * noise) if base else spread * noise
        out[name] = __import__('jax').numpy.asarray(drawn.astype(out[name].dtype))
    for name, factor in factors.items():
        out[name] = (out[name] * factor).astype(out[name].dtype)
    return out
```

```python
from contextlib import ExitStack

import concourse.bass as bass
from concourse import mybir

ALU = mybir.AluOpType
ACT = mybir.ActivationFunctionType
F32 = mybir.dt.float32
F32R = mybir.dt.float32r
U32 = mybir.dt.uint32
AX = mybir.AxisListType

P = 128
RING = 3
AHEAD = 2
GRID_W, KH, KW = 64, 8, 16
CHUNK = 128
LEVELS = (64, 32, 16, 8)
BASE = 8
NL = len(LEVELS) + 2
EPS, F_MIN, NEG = 1e-6, 1e-6, -1e30
HQ, HF, HB, HI, HG, NQ, NK, NV, NG = range(9)


def build_kernel(nc, x, p, norm_g, w_in, hgrn_lb, hgrn_onorm, na_qnorm, na_knorm, na_rpb,
                 w_branch_a, w_branch_b, w_out, ple_norm, w_ple_gate, w_ple, out):
    S, D = x.shape[1], x.shape[2]
    HW = w_branch_a.shape[1]
    H = HW // P
    PLE = p.shape[3]
    NT, KT, PT = S // P, D // P, PLE // P
    NR, NC = 2 * KH - 1, 2 * KW - 1
    ROWS = S // GRID_W
    assert S == 512 and D == 2048 and H == 8 and ROWS == KH and PT == 2
    SCALE = float(P) ** -0.5
    COL = [0, 2 * HW, 3 * HW, HW, 4 * HW, 5 * HW, 6 * HW, 7 * HW, 8 * HW]
    MA, MB = 9 * HW, 9 * HW + D
    NU = 18
    U_MERGE = H * NU
    U_OUT = U_MERGE + 6 * KT
    U_PLE = U_OUT + 6 * 4
    U_END = U_PLE + 6 * 4
    OUT_KT = [3, 3, 3, 3, 2, 2]
    DREAD = {HQ: 1, HG: 2, NQ: 3, NK: 4, NG: 5}

    x_v = x[0].rearrange("(t p) d -> p t d", p=P)
    out_v = out[0].rearrange("(t p) d -> p t d", p=P)
    p_v = p[0, 0].rearrange("(t p) e -> p t e", p=P)
    win_v = w_in[0].rearrange("(k p) n -> p k n", p=P)
    wa_v = w_branch_a[0].rearrange("(k p) n -> p k n", p=P)
    wb_v = w_branch_b[0].rearrange("(k p) n -> p k n", p=P)
    wo_v = w_out[0].rearrange("(k p) n -> p k n", p=P)
    wg_v = w_ple_gate[0].rearrange("(k p) n -> p k n", p=P)
    wp_v = w_ple[0].rearrange("(k p) n -> p k n", p=P)
    pn_v = ple_norm[0].rearrange("(c f p) -> c p f", p=P, f=4)

    z_dram = nc.dram_tensor("z_dram", [2 * H, P, S], F32, kind="Internal").ap()
    y_dram = nc.dram_tensor("y_dram", [KT, P, S], F32, kind="Internal").ap()
    x2_dram = nc.dram_tensor("x2_dram", [4, P, NT * 512], F32, kind="Internal").ap()
    x2t_dram = nc.dram_tensor("x2t_dram", [KT, P, S], F32, kind="Internal").ap()
    rpb_dram = nc.dram_tensor("rpb_dram", [H, GRID_W * NR * P], F32, kind="Internal").ap()

    with ExitStack() as ctx:
        ctx.enter_context(nc.allow_non_contiguous_dma(reason="norm weights, one element per partition"))

        def sb(name, shape, dt=F32, where=ctx):
            return where.enter_context(nc.sbuf_tensor(name, shape, dt))

        def sem(name):
            return ctx.enter_context(nc.semaphore(name))

        act_hi = sb("act_hi", [P, KT, S], F32R)
        act_lo = sb("act_lo", [P, KT, S], F32R)
        w_raw = sb("w_raw", [P, RING, 1536])
        w_hi = sb("w_hi", [P, RING, 1536], F32R)
        w_lo = sb("w_lo", [P, RING, 1536], F32R)
        ident = sb("ident", [P, P])
        mean_w = sb("mean_w", [P, P])
        cols = sb("cols", [P, 4])
        norm_c = sb("norm_c", [P, KT])
        eps_c = sb("eps_c", [P, 1])
        stat = sb("stat", [P, 4, NT])
        low = sb("low", [P, H, 4])
        low_h = sb("low_h", [P, 4])
        reset = sb("reset", [P, S])
        m_lev = sb("m_lev", [P, 2, len(LEVELS), CHUNK // 2])
        m_base = sb("m_base", [P, 2, CHUNK])
        m_win = sb("m_win", [P, GRID_W])
        rpb_pad = sb("rpb_pad", [P, P])
        mm_ps = ctx.enter_context(nc.psum_tensor("mm_ps", [P, 3, 512], F32))
        ax_ps = ctx.enter_context(nc.psum_tensor("ax_ps", [P, 5, 512], F32))

        with ExitStack() as first:
            x_in = sb("x_in", [P, NT, D], where=first)
            x_sq = sb("x_sq", [P, D], where=first)
            lb_col = sb("lb_col", [P, 4, 2 * H], where=first)
        with ExitStack() as heads:
            logf = sb("logf", [P, 2, S], where=heads)
            key = sb("key", [P, 2, S], where=heads)
            qry = sb("qry", [P, S], where=heads)
            cum = sb("cum", [P, 2, S], where=heads)
            dif = sb("dif", [P, 2, S], where=heads)
            lev = sb("lev", [P, len(LEVELS), S], where=heads)
            base_q = sb("base_q", [P, S], where=heads)
            base_k = sb("base_k", [P, S], where=heads)
            st_q = sb("st_q", [P, 2, S], where=heads)
            st_k = sb("st_k", [P, S], where=heads)
            st_kt = sb("st_kt", [P, 3 * P], where=heads)
            tot = sb("tot", [P, 2, NT], where=heads)
            state = sb("state", [P, 2, 3, P], where=heads)
            att = sb("att", [P, 2, S], where=heads)
            val = sb("val", [P, S], where=heads)
            gate = sb("gate", [P, S], where=heads)
            z_a = sb("z_a", [P, S], where=heads)
            v_t = sb("v_t", [P, S], where=heads)
            sig = sb("sig", [P, S], where=heads)
            sqr = sb("sqr", [P, S], where=heads)
            rms = sb("rms", [P, S], where=heads)
            n_q = sb("n_q", [P, S], where=heads)
            n_k = sb("n_k", [P, S], where=heads)
            n_v = sb("n_v", [P, S], where=heads)
            n_gate = sb("n_gate", [P, S], where=heads)
            bias = sb("bias", [P, (NR - 1) * GRID_W], where=heads)
            prob = sb("prob", [P, 2, S], where=heads)
            prob_t = sb("prob_t", [P, 2, S], where=heads)
            soft = sb("soft", [P, 4, NT], where=heads)
            z_b = sb("z_b", [P, S], where=heads)
        with ExitStack() as merge:
            g_ab = sb("g_ab", [P, 2, 2, S], where=merge)
            za_hi = sb("za_hi", [P, H, S], F32R, where=merge)
            za_lo = sb("za_lo", [P, H, S], F32R, where=merge)
            back = sb("back", [P, 2, 2, S], where=merge)
            zb_hi = sb("zb_hi", [P, H, S], F32R, where=merge)
            zb_lo = sb("zb_lo", [P, H, S], F32R, where=merge)
            y_out = sb("y_out", [P, S], where=merge)
            z_hi, z_lo = (za_hi, zb_hi), (za_lo, zb_lo)
        with ExitStack() as last:
            p_in = sb("p_in", [P, NT, PLE], where=last)
            p_hi = sb("p_hi", [P, PT, S], F32R, where=last)
            p_lo = sb("p_lo", [P, PT, S], F32R, where=last)
            xg = sb("xg", [P, NT, 512], where=last)
            x2g = sb("x2g", [P, NT, 512], where=last)
            x2t = sb("x2t", [P, 4, S], where=last)
            sb("below_back", [P, 1024], where=last)
            sb("under_back", [P, 2 * 2 * S], where=last)
            junk = sb("junk", [P, 512], where=last)
            pn_c = sb("pn_c", [P, 4], where=last)
            ssq = sb("ssq", [P, NT], where=last)
            p_w = sb("p_w", [P, NT, 512], where=last)
            g_sig = sb("g_sig", [P, NT, 512], where=last)
            res = sb("res", [P, NT, 512], where=last)

        raw_ready = [sem(f"raw_ready{s}") for s in range(RING)]
        pw_raw = sem("pw_raw")
        hi_done, lo_done, unit_done, acc_done = (sem(n) for n in ("hi_done", "lo_done", "unit_done", "acc_done"))
        x_ready = [sem(f"x_ready{t}") for t in range(NT)]
        const_in, lb_in, rpb_in, rpb_out = (sem(n) for n in ("const_in", "lb_in", "rpb_in", "rpb_out"))
        pool_step, pool_ready, lb_step, eps_ready = (
            sem(n) for n in ("pool_step", "pool_ready", "lb_step", "eps_ready"))
        x_sumsq, x_root, x_recip, x_normed = (sem(n) for n in ("x_sumsq", "x_root", "x_recip", "x_normed"))
        h_turned, h_hi, h_lo = (sem(n) for n in ("h_turned", "h_hi", "h_lo"))
        tile_act, tile_dve, low_ready, att_zero = (sem(n) for n in ("tile_act", "tile_dve", "low_ready", "att_zero"))
        att_part = [sem(f"att_part{l}") for l in range(len(LEVELS))]
        forget, key_ready, log_ready, cum_ready = (sem(n) for n in ("forget", "key_ready", "log_ready", "cum_ready"))
        dif_ready, dec_ready, q_side, k_side = (sem(n) for n in ("dif_ready", "dec_ready", "q_side", "k_side"))
        intra_done, att_ready, kt_ready = (sem(n) for n in ("intra_done", "att_ready", "kt_ready"))
        upd_done, state_ready, o_done, osq_ready = (sem(n) for n in ("upd_done", "state_ready", "o_done", "osq_ready"))
        ms_done, root_ready, rinv_ready, normed = (sem(n) for n in ("ms_done", "root_ready", "rinv_ready", "normed"))
        za_last, zb_last, x2_last, x2t_last = (sem(n) for n in ("za_last", "zb_last", "x2_last", "x2t_last"))
        vt_done, val_ready = sem("vt_done"), sem("val_ready")
        za_part, za_stored, zb_ready, zb_stored = (sem(n) for n in ("za_part", "za_stored", "zb_ready", "zb_stored"))
        bias_in, bias_ready = sem("bias_in"), sem("bias_ready")
        s_done, s_biased, s_max, s_neg = (sem(n) for n in ("s_done", "s_biased", "s_max", "s_neg"))
        e_done, e_recip, p_ready = (sem(n) for n in ("e_done", "e_recip", "p_ready"))
        pt_done, pt_ready, pv_done = (sem(n) for n in ("pt_done", "pt_ready", "pv_done"))
        z_in = [sem("z_in0"), sem("z_in1")]
        z_hi_done, z_lo_done, gate_ready = (sem(n) for n in ("z_hi_done", "z_lo_done", "gate_ready"))
        y_part, y_ready, y_stored = (sem(n) for n in ("y_part", "y_ready", "y_stored"))
        a_in = [sem("a_in0"), sem("a_in1")]
        a_hi_done, a_lo_done = sem("a_hi_done"), sem("a_lo_done")
        p_landed, p_turned, p_hi_done, p_lo_done = (sem(n) for n in ("p_landed", "p_turned", "p_hi_done", "p_lo_done"))
        xg_in, pn_in, x2_ready, x2_sq, ss_sum = (sem(n) for n in ("xg_in", "pn_in", "x2_ready", "x2_sq", "ss_sum"))
        x2_turned, x2t_ready, x2_stored, x2t_stored = (
            sem(n) for n in ("x2_turned", "x2t_ready", "x2_stored", "x2t_stored"))
        rstd_root, rstd_ready, pw_ready, x2_in = (sem(n) for n in ("rstd_root", "rstd_ready", "pw_ready", "x2_in"))
        g_ready, gp_ready, res_ready, out_stored = (sem(n) for n in ("g_ready", "gp_ready", "res_ready", "out_stored"))

        POOL_STEPS = 12 + 2 * (2 * len(LEVELS) + 2)

        block = ctx.enter_context(nc.Block())

        class Units:

            def __init__(self, first, step=0, r=0):
                self.first, self.step, self.r = first, step, r

            def num(self, i):
                return self.r * self.step + (self.first + i)

            def slot(self, i):
                return (self.first + i) % RING

            def fills(self, i):
                return self.r * (self.step // RING) + ((self.first + i) // RING + 1)

            def reuses(self, i):
                return not (isinstance(self.r, int) and self.num(i) < RING)

        def load_w(sp, us, i, src):
            if us.reuses(i):
                sp.wait_ge(lo_done, us.num(i) - (RING - 1))
            k, n = src.shape[1], src.shape[2]
            dst = w_raw[:, us.slot(i), 0:k * n].rearrange("p (k n) -> p k n", k=k)
            sp.dma_start(dst, src).then_inc(raw_ready[us.slot(i)], 16)

        def split_hi(act, us, i, width=1024):
            s = us.slot(i)
            act.wait_ge(raw_ready[s], us.fills(i) * 16)
            if us.reuses(i):
                act.wait_ge(unit_done, us.num(i) - (RING - 1))
            nc.scalar.activation(w_hi[:, s, 0:width], w_raw[:, s, 0:width], ACT.Copy).then_inc(hi_done, 1)

        def split_lo(dve, us, i, width=1024):
            s = us.slot(i)
            dve.wait_ge(hi_done, us.num(i) + 1)
            if us.reuses(i):
                dve.wait_ge(unit_done, us.num(i) - (RING - 1))
            nc.vector.tensor_tensor(w_lo[:, s, 0:width], w_raw[:, s, 0:width],
                                    w_hi[:, s, 0:width].bitcast(F32), ALU.subtract).then_inc(lo_done, 1)

        def out_width(i):
            return OUT_KT[i % 6] * 512

        def halves(ap, m, d, side):
            h = int((side == "q") == (d == 0))
            return ap.rearrange("p (b h u) -> p b h u", h=2, u=m)[:, :, h, :]

        def reference(ap, l, d):
            if l < len(LEVELS):
                w, r = 2 * LEVELS[l], LEVELS[l] - 1 + d
            elif l == len(LEVELS):
                w, r = BASE, BASE // 2 - 1 + d
            else:
                w, r = CHUNK, (CHUNK - 1) * (1 - d)
            v = ap.rearrange("p (b w) -> p b w", w=w)
            return v, v[:, :, r:r + 1].to_broadcast([P, S // w, w]), w

        ST = [dict(q=slice(CHUNK, S), k=slice(0, S - CHUNK)), dict(q=slice(0, S - CHUNK), k=slice(CHUNK, S))]
        FEED = [[0, 1, 2], [3, 2, 1]]

        def rpb_rows(h, r2):
            v = rpb_dram[bass.ds(h, 1), (1 - r2) * P + GRID_W - 1:GRID_W * NR * P]
            return bass.AP(tensor=v.tensor, offset=v.offset, ap=[[NR * P - 1, GRID_W], [P, NR - 1], [1, GRID_W]])

        def acc(t):
            return mm_ps[:, t, :] if t < 3 else ax_ps[:, 0, :]

        def acc_full(eng, us, g, t):
            if t < NT - 1:
                eng.wait_ge(acc_done, g * (NT - 1) + (t + 1))
            else:
                eng.wait_ge(unit_done, us.num(6))

        def branch_ps(slot, b):
            return mm_ps[:, 2, :] if slot == 0 and b == 0 else ax_ps[:, 0 if slot == 0 else 1 + b, :]

        @block.sync
        def _(sp):
            us = Units(0)
            for t in range(NT):
                sp.dma_start(x_in[:, t, :], x_v[:, t, :]).then_inc(x_ready[t], 16)
            for i in range(2):
                load_w(sp, us, i, win_v[:, 8 * i:8 * i + 8, COL[HQ]:COL[HQ] + P])

            def head(h):
                us = Units(0, NU, h)
                for i in range(NU):
                    if isinstance(h, int) and i < 2:
                        continue
                    load_w(sp, us, i, win_v[:, 8 * (i % 2):8 * (i % 2) + 8, bass.ds(h * P + COL[i // 2], P)])
                    if i == 7 and not isinstance(h, int):
                        sp.wait_ge(normed, 3 * h)
                        sp.dma_start(z_dram[bass.ds(h - 1, 1)].rearrange("a p s -> p (a s)"), z_a[:, :]).then_inc(za_stored, 16)
                    if i == 10:
                        if isinstance(h, int):
                            sp.wait_ge(rpb_out, 16 * H)
                            sp.wait_ge(h_lo, KT)
                        else:
                            sp.wait_ge(s_biased, 4 * h)
                        for r2 in range(2):
                            src = rpb_rows(h, r2)
                            dst = bias[r2 * GRID_W:(r2 + 1) * GRID_W, :].rearrange("c (d j) -> c d j", j=GRID_W)
                            sp.dma_start(dst, src).then_inc(bias_in, 16)
                    if i == 13 and not isinstance(h, int):
                        sp.wait_ge(zb_ready, h)
                        sp.dma_start(z_dram[bass.ds(h + (H - 1), 1)].rearrange("a p s -> p (a s)"), z_b[:, :]).then_inc(zb_stored, 16)

            head(0)
            with sp.Fori(1, H) as h:
                head(h)

            us = Units(U_MERGE)
            for i in range(8):
                c = (MA if i % 4 < 2 else MB) + P * (i // 4)
                load_w(sp, us, i, win_v[:, 8 * (i % 2):8 * (i % 2) + 8, c:c + P])

            def branches(us, i, n):
                load_w(sp, us, i, wa_v[:, :, bass.ds(n * P, P)])
                load_w(sp, us, i + 1, wb_v[:, :, bass.ds(n * P, P)])

            def store_y(n):
                sp.wait_ge(y_ready, n + 1)
                sp.dma_start(y_dram[bass.ds(n, 1)].rearrange("a p s -> p (a s)"), y_out[:, :]).then_inc(y_stored, 16)

            def merge_pair(r, is_first=False):
                us = Units(U_MERGE + 8, 12, r)
                for e in range(2):
                    branches(us, 6 * e, r * 2 + e)
                    for i in range(4):
                        load_w(sp, us, 6 * e + 2 + i, win_v[:, 8 * (i % 2):8 * (i % 2) + 8,
                               bass.ds(r * (2 * P) + ((MA if i < 2 else MB) + (2 + e) * P), P)])
                        if i == 0 and not (is_first and e == 0):
                            store_y(r * 2 + (e - 1))

            merge_pair(0, is_first=True)
            with sp.Fori(1, KT // 2 - 1) as r:
                merge_pair(r)
            us = Units(U_OUT - 4)
            branches(us, 0, KT - 2)
            store_y(KT - 3)
            branches(us, 2, KT - 1)

            def out_group(c, is_first=False):
                us = Units(U_OUT, 6, c)
                for i, kn in enumerate(OUT_KT):
                    k = sum(OUT_KT[:i])
                    load_w(sp, us, i, wo_v[:, k:k + kn, bass.ds(c * 512, 512)])
                    if is_first and i == 1:
                        store_y(KT - 2)
                    if is_first and i == 3:
                        store_y(KT - 1)
                if not is_first:
                    sp.wait_ge(x2_ready, 4 * c)
                    sp.dma_start(x2_dram[bass.ds(c - 1, 1)].rearrange("a p s -> p (a s)"),
                                 x2g[:, :, :].rearrange("p t j -> p (t j)")).then_inc(x2_stored, 16)
                    sp.wait_ge(x2t_ready, 4 * c)
                    sp.dma_start(x2t_dram[bass.ds(4 * c - 4, 4)].rearrange("f p s -> p f s"),
                                 x2t[:, :, :]).then_inc(x2t_stored, 16)
                sp.dma_start(xg[:, :, :], x_v[:, :, bass.ds(c * 512, 512)]).then_inc(xg_in, 16)
                sp.dma_start(pn_c[:, :], pn_v[bass.ds(c, 1)].rearrange("c p f -> p (c f)")).then_inc(pn_in, 16)

            out_group(0, is_first=True)
            with sp.Fori(1, 4) as c:
                out_group(c)

            def ple_unit(us, i, c):
                if i == 0:
                    sp.wait_ge(lo_done, us.num(0) - (RING - 1))
                    dst = w_raw[:, us.slot(0), 0:PT * 512].rearrange("p (k n) -> p k n", k=PT)
                    sp.dma_start(dst, wp_v[:, :, bass.ds(c * 512, 512)]).then_inc(pw_raw, 16)
                    dst = w_raw[:, us.slot(0), PT * 512:1536].rearrange("p (k n) -> p k n", k=1)
                    sp.dma_start(dst, wg_v[:, 0:1, bass.ds(c * 512, 512)]).then_inc(raw_ready[us.slot(0)], 16)
                else:
                    load_w(sp, us, i, wg_v[:, 3 * i - 2:3 * i + 1, bass.ds(c * 512, 512)])

            def store_out(c):
                for t in range(NT):
                    sp.wait_ge(res_ready, 4 * c + (t + 1))
                    sp.dma_start(out_v[:, t, bass.ds(c * 512, 512)], res[:, t, :]).then_inc(out_stored, 16)

            def ple_group(c, is_first=False):
                us = Units(U_PLE, 6, c)
                for i in range(6):
                    ple_unit(us, i, c)
                if is_first:
                    sp.wait_ge(x2_ready, 16)
                    sp.wait_ge(x2_stored, 16 * 3)
                    sp.wait_ge(x2_last, 16)
                else:
                    store_out(c - 1)
                sp.dma_start(xg[:, :, :].rearrange("p t j -> p (t j)"),
                             x2_dram[bass.ds(c, 1)].rearrange("a p s -> p (a s)")).then_inc(x2_in, 16)

            ple_group(0, is_first=True)
            with sp.Fori(1, 4) as c:
                ple_group(c)
            store_out(3)
            sp.wait_ge(out_stored, 16 * 16)

        @block.gpsimd
        def _(pool):
            steps = [0]

            def link(ins):
                steps[0] += 1
                ins.then_inc(pool_step, 1)
                pool.wait_ge(pool_step, steps[0])

            def keep(v, pattern, base, cm, fill, compare=ALU.is_ge):
                link(nc.gpsimd.affine_select(out=v, in_=v, compare_op=compare, fill=fill, base=base,
                                             pattern=pattern, channel_multiplier=cm))

            link(nc.gpsimd.memset(ident[:, :], 0.0))
            keep(ident[:, :], [[-1, P]], 0, 1, 1.0, ALU.not_equal)
            nc.gpsimd.memset(mean_w[:, :], 1.0 / P).then_inc(pool_ready, 1)
            pool.dma_start(norm_c[:, :], norm_g[0].rearrange("(k p) -> p k", p=P)).then_inc(const_in, 16)
            pool.dma_start(cols[:, 0:1], hgrn_onorm.rearrange("a p -> p a")).then_inc(const_in, 16)
            pool.dma_start(cols[:, 1:2], na_qnorm.rearrange("a p -> p a")).then_inc(const_in, 16)
            pool.dma_start(cols[:, 2:3], na_knorm.rearrange("a p -> p a")).then_inc(const_in, 16)
            for d in range(2):
                pool.dma_start(lb_col[:, 0, d * H:(d + 1) * H],
                               hgrn_lb[0, d].rearrange("(h p) -> p h", p=P)).then_inc(lb_in, 16)
            link(nc.gpsimd.memset(rpb_pad[:, :], 0.0))
            pool.dma_start(rpb_pad[0:H * NR, GRID_W - KW:GRID_W - KW + NC],
                           na_rpb[0].rearrange("h r c -> (h r) c")).then_inc(rpb_in, 16)
            pool.wait_ge(rpb_in, 16)
            for h in range(H):
                src = rpb_pad[h * NR:(h + 1) * NR, :].rearrange("r (a x) -> r a x", a=1).to_broadcast([NR, GRID_W, P])
                dst = rpb_dram[h].rearrange("(c r x) -> r c x", c=GRID_W, x=P)
                pool.dma_start(dst, src).then_inc(rpb_out, 16)
            link(nc.gpsimd.memset(reset[:, :], 1.0))
            link(nc.gpsimd.memset(reset[:, :].rearrange("p (c u) -> p c u", u=CHUNK)[:, :, 0:1], 0.0))
            link(nc.gpsimd.memset(m_lev[:, :, :, :], 1.0))
            link(nc.gpsimd.memset(m_base[:, :, :], 1.0))
            for d in range(2):
                for l, m in enumerate(LEVELS):
                    nb, ko = CHUNK // (2 * m), m * d
                    v = m_lev[:, d, l, :].rearrange("p (b u) -> p b u", u=m)
                    keep(v, [[-2 * m, nb], [0, m]], -ko, 1, 0.0)
                    keep(v, [[2 * m, nb], [0, m]], ko + m - 1, -1, 0.0)
                v = m_base[:, d, :].rearrange("p (b u) -> p b u", u=BASE)
                nb = CHUNK // BASE
                keep(v, [[-BASE, nb], [-d, BASE]], 0, 1, 0.0)
                keep(v, [[BASE, nb], [1 - d, BASE]], (BASE - 1) * d, -1, 0.0)
            link(nc.gpsimd.memset(m_win[:, :], 0.0))
            for r2 in range(2):
                rows = slice(r2 * GRID_W, (r2 + 1) * GRID_W)
                keep(m_win[rows, 0:GRID_W - KW], [[1, GRID_W - KW]], KW // 2, -1, NEG)
                keep(m_win[rows, KW:GRID_W], [[-1, GRID_W - KW]], KW // 2 - 1 - KW, 1, NEG)

            assert steps[0] == POOL_STEPS

            def key_scale(h, d):
                pool.wait_ge(tile_act, 9 * h + (HF + d + 1))
                pool.wait_ge(low_ready, h + 1)
                nc.gpsimd.tensor_tensor(key[:, d, :], key[:, d, :], low_h[:, 2 + d:3 + d].to_broadcast([P, S]),
                                        ALU.mult).then_inc(key_ready, 1)

            def key_sides(h, d):
                pool.wait_ge(key_ready, 2 * h + (d + 1))
                for l in range(NL):
                    pool.wait_ge(dec_ready, 12 * h + (6 * d + l + 1))
                    if l < len(LEVELS):
                        o, k = (halves(v, LEVELS[l], d, "k") for v in (lev[:, l, :], key[:, d, :]))
                    elif l == len(LEVELS):
                        o, k = base_k[:, :], key[:, d, :]
                    else:
                        o, k = st_k[:, ST[d]["k"]], key[:, d, ST[d]["k"]]
                    nc.gpsimd.tensor_tensor(o, o, k, ALU.mult).then_inc(k_side, 1)

            def head(h):
                for d in range(2):
                    key_scale(h, d)
                    key_sides(h, d)
                pool.wait_ge(bias_in, 32 * h + 32)
                v = bias[:, :].rearrange("p (d j) -> p d j", j=GRID_W)
                w = m_win[:, :].rearrange("p (a j) -> p a j", a=1).to_broadcast([P, NR - 1, GRID_W])
                nc.gpsimd.tensor_tensor(v, v, w, ALU.add).then_inc(bias_ready, 1)

            head(0)
            with pool.Fori(1, H) as h:
                head(h)

            pool.wait_ge(za_stored, 16 * (H - 1))
            pool.wait_ge(za_part, H)
            for q in range(H):
                if q == 2:
                    pool.wait_ge(normed, 3 * H)
                    pool.dma_start(z_dram[H - 1], z_a[:, :]).then_inc(za_last, 16)
                if q == 3:
                    pool.wait_ge(za_last, 16)
                if q == 4:
                    pool.wait_ge(zb_stored, 16 * (H - 1))
                if q == 6:
                    pool.wait_ge(zb_ready, H)
                    pool.dma_start(z_dram[2 * H - 1], z_b[:, :]).then_inc(zb_last, 16)
                if q == 7:
                    pool.wait_ge(zb_last, 16)
                if q >= 2:
                    pool.wait_ge(z_lo_done, 2 * (q - 1))
                pool.dma_start(back[:, q % 2], z_dram[2 * q:2 * q + 2].rearrange("f p s -> p f s")).then_inc(z_in[q % 2], 16)

            def bring(n, src):
                if n >= 2:
                    pool.wait_ge(a_lo_done, 2 * (n - 1))
                q = n % (KT // 2)
                pool.dma_start(back[:, n % 2], src[2 * q:2 * q + 2].rearrange("f p s -> p f s")).then_inc(a_in[n % 2], 16)

            for n in range(KT // 2):
                pool.wait_ge(y_stored, 16 * (KT - 3 if n < KT // 2 - 2 else KT - 2 if n < KT // 2 - 1 else KT))
                bring(n, y_dram)
            pool.wait_ge(y_ready, KT)
            pool.dma_start(p_in[:, :, :], p_v).then_inc(p_landed, 16)
            pool.wait_ge(x2t_stored, 16 * 3)
            for n in range(KT // 2, KT):
                if n == KT // 2 + 2:
                    pool.wait_ge(x2_ready, 16)
                    pool.dma_start(x2_dram[3], x2g[:, :, :].rearrange("p t j -> p (t j)")).then_inc(x2_last, 16)
                if n == KT - 2:
                    pool.wait_ge(x2t_ready, 16)
                    pool.dma_start(x2t_dram[12:16].rearrange("f p s -> p f s"), x2t[:, :, :]).then_inc(x2t_last, 16)
                    pool.wait_ge(x2t_last, 16)
                bring(n, x2t_dram)
            pool.wait_ge(x2_last, 16)

        @block.scalar
        def _(act):
            A = nc.scalar.activation

            act.wait_ge(eps_ready, 1)
            for t in range(NT):
                act.wait_ge(x_ready[t], 16)
                if t:
                    act.wait_ge(x_sumsq, t)
                A(x_sq[:, :], x_in[:, t, :], ACT.Square, accum_out=stat[:, 0, t:t + 1]).then_inc(x_sumsq, 1)
                act.wait_ge(x_sumsq, t + 1)
                A(stat[:, 1, t:t + 1], stat[:, 0, t:t + 1], ACT.Sqrt, bias=eps_c[:, :], scale=1.0 / D).then_inc(x_root, 1)
            split_hi(act, Units(0), 0)
            split_hi(act, Units(0), 1)
            act.wait_ge(const_in, 64)
            for k in range(KT):
                act.wait_ge(h_turned, k + 1)
                A(act_hi[:, k, :], ax_ps[:, k % 5, :], ACT.Copy, scale=norm_c[:, k:k + 1]).then_inc(h_hi, 1)
            act.wait_ge(lb_step, 1)
            A(lb_col[:, 2, :], lb_col[:, 1, :], ACT.Exp).then_inc(lb_step, 1)

            def chain(h, d):
                act.wait_ge(forget, 4 * h + (2 * d + 2))
                A(logf[:, d, :], logf[:, d, :], ACT.Ln).then_inc(log_ready, 1)
                if not (isinstance(h, int) and d == 0):
                    act.wait_ge(intra_done, 2 * h + d)
                for l in range(NL):
                    act.wait_ge(dif_ready, 12 * h + (6 * d + l + 1))
                    e = dif[:, l % 2, :]
                    if l < len(LEVELS):
                        for side, sign in (("q", 1.0), ("k", -1.0)):
                            last = A(halves(lev[:, l, :], LEVELS[l], d, side), halves(e, LEVELS[l], d, side),
                                     ACT.Exp, scale=sign)
                    elif l == len(LEVELS):
                        A(base_q[:, :], e, ACT.Exp)
                        last = A(base_k[:, :], e, ACT.Exp, scale=-1.0)
                    else:
                        if not isinstance(h, int):
                            act.wait_ge(o_done, h)
                        v = cum[:, d, :].rearrange("p (c u) -> p c u", u=CHUNK)
                        r = (CHUNK - 1) * (1 - d)
                        A(tot[:, d, :], v[:, :, r], ACT.Exp)
                        A(st_q[:, d, ST[d]["q"]], cum[:, d, ST[d]["q"]], ACT.Exp)
                        last = A(st_k[:, ST[d]["k"]], dif[:, l % 2, ST[d]["k"]], ACT.Exp, scale=-1.0)
                    last.then_inc(dec_ready, 1)

            def keys_t(h, d):
                act.wait_ge(intra_done, 2 * h + (d + 1))
                if not (isinstance(h, int) and d == 0):
                    act.wait_ge(upd_done, 2 * h + d)
                A(st_kt[:, :], ax_ps[:, 3, 0:3 * P], ACT.Copy).then_inc(kt_ready, 1)

            def root(h, m):
                act.wait_ge(ms_done, 3 * h + (m + 1))
                if not (isinstance(h, int) and h == 0 and m == 0):
                    act.wait_ge(normed, 3 * h + m)
                A(rms[:, :], ax_ps[:, m, :], ACT.Sqrt, bias=eps_c[:, :]).then_inc(root_ready, 1)

            def tile(h, j):
                ps = mm_ps[:, j % 3, :]
                act.wait_ge(unit_done, NU * h + (2 * j + 2))
                if j in (HF, HB):
                    A(logf[:, j - HF, :], ps, ACT.Sigmoid)
                    last = A(key[:, j - HF, :], ps, ACT.Sigmoid, scale=-1.0)
                elif j in (HI, NV):
                    if j == NV or not isinstance(h, int):
                        act.wait_ge(vt_done, 2 * h + (1 if j == NV else 0))
                    last = A(v_t[:, :], ps, ACT.Copy)
                elif j in (NQ, NK):
                    if j == NK or not isinstance(h, int):
                        act.wait_ge(ms_done, 3 * h + (1 if j == NK else 0))
                    last = A(sqr[:, :], ps, ACT.Square)
                else:
                    if j != HQ or not isinstance(h, int):
                        act.wait_ge(tile_dve, 5 * h + {HQ: 0, HG: 1, NG: 2}[j])
                    last = A(sig[:, :], ps, ACT.Sigmoid)
                last.then_inc(tile_act, 1)

            def late(i, g):
                if i == 0:
                    root(g, 2)
                    tile(g, NG)
                    act.wait_ge(vt_done, 2 * g + 2)
                    A(n_v[:, :], ax_ps[:, 3, :], ACT.Copy).then_inc(val_ready, 1)
                if 1 <= i <= 4:
                    t = i - 1
                    act.wait_ge(s_neg, 4 * g + (t + 1))
                    A(prob[:, t % 2, :], prob[:, t % 2, :], ACT.Exp, bias=soft[:, 1, t:t + 1],
                      accum_out=soft[:, 2, t:t + 1]).then_inc(e_done, 1)
                if 3 <= i <= 6:
                    t = i - 3
                    act.wait_ge(pt_done, 4 * g + (t + 1))
                    if t >= 2:
                        act.wait_ge(pv_done, 4 * g + (t - 1))
                    A(prob_t[:, t % 2, :], ax_ps[:, 2 + t % 2, :], ACT.Copy).then_inc(pt_ready, 1)

            def head(h):
                us = Units(0, NU, h)
                for i in range(NU):
                    split_hi(act, us, i + AHEAD)
                    if not isinstance(h, int):
                        late(i, h - 1)
                    if i == 9:
                        keys_t(h, 0)
                    if i == 12:
                        keys_t(h, 1)
                    if i == 10:
                        act.wait_ge(vt_done, 2 * h + 1)
                        A(val[:, :], ax_ps[:, 3, :], ACT.Copy).then_inc(val_ready, 1)
                    if i in (14, 16):
                        root(h, (i - 14) // 2)
                    if i == 16:
                        act.wait_ge(o_done, h + 1)
                        act.wait_ge(ms_done, 3 * h + 2)
                        A(sqr[:, :], ax_ps[:, 4, :], ACT.Square).then_inc(osq_ready, 1)
                    if i % 2 == 0 and i >= 2:
                        tile(h, i // 2 - 1)
                    if i == 5:
                        chain(h, 0)
                    if i == 9:
                        chain(h, 1)

            head(0)
            with act.Fori(1, H) as h:
                head(h)

            def merge_gate(n, b, slot, done):
                act.wait_ge(unit_done, done)
                if not (isinstance(n, int) and n < 2):
                    act.wait_ge(y_ready, n - 1)
                A(g_ab[:, slot, b, :], mm_ps[:, b, :], ACT.Sigmoid).then_inc(gate_ready, 1)

            def z_hi_tiles(k0, k1):
                for k in range(k0, k1):
                    act.wait_ge(z_in[k // 2 % 2], 16 * (k // 4 + 1))
                    A(z_hi[k // H][:, k % H, :], back[:, k // 2 % 2, k % 2, :], ACT.Copy).then_inc(z_hi_done, 1)

            us = Units(U_MERGE)
            for i in range(8):
                split_hi(act, us, i + AHEAD)
                late(i, H - 1)
                if i:
                    z_hi_tiles(i if i > 1 else 0, i + 1)
                if i in (2, 4):
                    merge_gate(0, i // 2 - 1, 0, us.num(i))
                if i == 6:
                    merge_gate(1, 0, 1, us.num(i))

            def merge_pair(r, is_first=False):
                us = Units(U_MERGE + 8, 12, r)
                for i in range(12):
                    split_hi(act, us, i + AHEAD)
                    if is_first and i == 0:
                        act.wait_ge(zb_ready, H)
                        z_hi_tiles(H, 2 * H)
                    if i in (0, 4, 6, 10):
                        n, b, s = {0: (1, 1, 1), 4: (2, 0, 0), 6: (2, 1, 0), 10: (3, 0, 1)}[i]
                        merge_gate(r * 2 + n, b, s, us.num(i))

            merge_pair(0, is_first=True)
            with act.Fori(1, KT // 2 - 1) as r:
                merge_pair(r)

            def act_hi_tiles(k0, k1, phase):
                for k in range(k0, k1):
                    n = phase * (KT // 2) + k // 2
                    act.wait_ge(a_in[n % 2], 16 * (n // 2 + 1))
                    A(act_hi[:, k, :], back[:, n % 2, k % 2, :], ACT.Copy).then_inc(a_hi_done, 1)

            us = Units(U_OUT - 4)
            for i in range(4):
                split_hi(act, us, i + AHEAD, 1024 if i < 2 else out_width(i - 2))
                if i == 0:
                    merge_gate(KT - 1, 1, 1, us.num(0))
                    act.wait_ge(unit_done, U_OUT - 4)
                act_hi_tiles(4 * i, min(4 * i + 4, 14), 0)

            def squares(c):
                for t in range(NT):
                    act.wait_ge(x2_ready, 4 * c + (t + 1))
                    if not (isinstance(c, int) and c == 0 and t == 0):
                        act.wait_ge(x2_sq, 4 * c + t)
                    if t == 0 and not (isinstance(c, int) and c == 0):
                        act.wait_ge(ss_sum, c + 1)
                    A(junk[:, :], x2g[:, t, :], ACT.Square, accum_out=ssq[:, t:t + 1]).then_inc(x2_sq, 1)

            def turn_out(c):
                act.wait_ge(pn_in, 16 * c + 16)
                for f in range(4):
                    act.wait_ge(x2_turned, 4 * c + (f + 1))
                    A(x2t[:, f, :], ax_ps[:, 1 + f, :], ACT.Copy, scale=pn_c[:, f:f + 1]).then_inc(x2t_ready, 1)

            def out_group(c, is_first=False):
                us = Units(U_OUT, 6, c)
                for i in range(6):
                    if i == 4 and isinstance(c, int) and c == 3:
                        act.wait_ge(pw_raw, 16)
                    split_hi(act, us, i + AHEAD, out_width(i + AHEAD))
                    if is_first and i == 1:
                        act_hi_tiles(14, KT, 0)
                    if is_first and i == 3:
                        for k in range(PT):
                            act.wait_ge(p_turned, k + 1)
                            A(p_hi[:, k, :], ax_ps[:, 1 + k, :], ACT.Copy).then_inc(p_hi_done, 1)
                    if not is_first and i == 1:
                        turn_out(c - 1)
                if not is_first:
                    act.wait_ge(x2t_stored, 16 * c)
                squares(c)

            out_group(0, is_first=True)
            with act.Fori(1, 3) as c:
                out_group(c)
            out_group(3)
            act.wait_ge(unit_done, U_PLE)
            act_hi_tiles(0, 4, 1)

            def ple_group(c, is_first=False, is_last=False):
                us = Units(U_PLE, 6, c)
                for i in range(6):
                    if not (is_last and i + AHEAD >= 6):
                        if i == 4:
                            act.wait_ge(pw_raw, 16 * c + 32)
                        split_hi(act, us, i + AHEAD, 1536)
                    if is_first and i == 1:
                        act.wait_ge(ss_sum, 5)
                        A(stat[:, 1, :], stat[:, 3, :], ACT.Sqrt, bias=eps_c[:, :], scale=1.0 / D).then_inc(rstd_root, 1)
                    if is_first and i == 2:
                        turn_out(3)
                    if is_first and i < 4:
                        act_hi_tiles(4 + 3 * i, 7 + 3 * i, 1)
                act.wait_ge(rstd_ready, 1)
                for t in range(NT):
                    acc_full(act, us, c + 4, t)
                    if not (isinstance(c, int) and c == 0):
                        act.wait_ge(res_ready, 4 * c - 3 + t)
                    A(g_sig[:, t, :], acc(t), ACT.Sigmoid, scale=stat[:, 2, t:t + 1]).then_inc(g_ready, 1)

            ple_group(0, is_first=True)
            with act.Fori(1, 3) as c:
                ple_group(c)
            ple_group(3, is_last=True)

        @block.vector
        def _(dve):
            TT, STT, TS = nc.vector.tensor_tensor, nc.vector.scalar_tensor_tensor, nc.vector.tensor_scalar
            nc.vector.memset(eps_c[:, :], EPS).then_inc(eps_ready, 1)
            for t in range(NT):
                dve.wait_ge(x_root, t + 1)
                nc.vector.reciprocal(stat[:, 2, t:t + 1], stat[:, 1, t:t + 1]).then_inc(x_recip, 1)
                dve.wait_ge(x_recip, t + 1)
                TS(x_in[:, t, :], x_in[:, t, :], stat[:, 2, t:t + 1], None, ALU.mult).then_inc(x_normed, 1)
            split_lo(dve, Units(0), 0)
            split_lo(dve, Units(0), 1)
            dve.wait_ge(const_in, 64)
            for k in range(KT):
                dve.wait_ge(h_hi, k + 1)
                STT(act_lo[:, k, :], ax_ps[:, k % 5, :], norm_c[:, k:k + 1], act_hi[:, k, :].bitcast(F32),
                    ALU.mult, ALU.subtract).then_inc(h_lo, 1)
            dve.wait_ge(lb_in, 32)
            TT(lb_col[:, 1, :], lb_col[:, 0, :], lb_col[:, 0, :], ALU.subtract).then_inc(lb_step, 1)
            dve.wait_ge(lb_step, 2)
            nc.vector.reciprocal(lb_col[:, 3, :], lb_col[:, 2, :]).then_inc(lb_step, 1)
            dve.wait_ge(lb_step, 3)
            TT(lb_col[:, 0, :], lb_col[:, 2, :], lb_col[:, 3, :], ALU.mult).then_inc(lb_step, 1)
            dve.wait_ge(lb_step, 4)
            v = lb_col[:, 0, :].rearrange("p (d h) -> p h d", d=2)
            TT(low[:, :, 0:2], v, v, ALU.subtract).then_inc(lb_step, 1)
            dve.wait_ge(lb_step, 5)
            TS(low[:, :, 2:4], low[:, :, 0:2], -1.0, 1.0, ALU.mult, ALU.add).then_inc(lb_step, 1)

            def forget_gate(h, d):
                dve.wait_ge(tile_act, 9 * h + (HF + d + 1))
                dve.wait_ge(low_ready, h + 1)
                TS(logf[:, d, :], logf[:, d, :], low_h[:, 2 + d:3 + d], low_h[:, d:d + 1],
                   ALU.mult, ALU.add).then_inc(forget, 1)
                dve.wait_ge(forget, 4 * h + (2 * d + 1))
                TS(logf[:, d, :], logf[:, d, :], F_MIN, None, ALU.max).then_inc(forget, 1)

            def chain(h, d):
                dve.wait_ge(log_ready, 2 * h + (d + 1))
                f, c = logf[:, d, :], cum[:, d, :]
                if d:
                    f, c = f[:, ::-1], c[:, ::-1]
                nc.vector.tensor_tensor_scan(c, reset[:, :], f, 0.0, ALU.mult, ALU.add).then_inc(cum_ready, 1)
                dve.wait_ge(cum_ready, 2 * h + (d + 1))

                def distance(l):
                    if not (isinstance(h, int) and d == 0 and l < 2):
                        dve.wait_ge(dec_ready, 12 * h + (6 * d + l - 1))
                    v, ref, w = reference(cum[:, d, :], l, d)
                    TT(dif[:, l % 2, :].rearrange("p (b w) -> p b w", w=w), v, ref, ALU.subtract).then_inc(dif_ready, 1)

                def query_side(l):
                    dve.wait_ge(dec_ready, 12 * h + (6 * d + l + 1))
                    if l < len(LEVELS):
                        o, q = (halves(v, LEVELS[l], d, "q") for v in (lev[:, l, :], qry[:, :]))
                    elif l == len(LEVELS):
                        o, q = base_q[:, :], qry[:, :]
                    else:
                        o, q = st_q[:, d, ST[d]["q"]], qry[:, ST[d]["q"]]
                    TT(o, o, q, ALU.mult).then_inc(q_side, 1)

                distance(0)
                distance(1)
                for l in range(NL):
                    query_side(l)
                    if l + 2 < NL:
                        distance(l + 2)

            def products(h, d):
                def place(l, o, k, s):
                    dve.wait_ge(pool_step, POOL_STEPS)
                    if l:
                        dve.wait_ge(att_part[l - 1], 2 * h + (d + 1))
                    else:
                        dve.wait_ge(intra_done, 2 * h + (d + 1))
                        if not isinstance(h, int):
                            dve.wait_ge(o_done, h)
                    nc.vector.copy_predicated(o, k, s).then_inc(att_part[l] if l < len(LEVELS) else att_ready, 1)

                for l, m in enumerate(LEVELS):
                    nb = CHUNK // (2 * m)
                    hq = 1 - d
                    o = att[:, d, :].rearrange("p (t b h u) -> p t b h u", t=NT, h=2, u=m)[:, :, :, hq, :]
                    s = ax_ps[:, l // 2, (l % 2) * 256:(l % 2) * 256 + 256].rearrange("p (t b u) -> p t b u", t=NT, u=m)
                    k = m_lev[:, d, l, :].bitcast(U32).rearrange("p (a b u) -> p a b u", a=1, u=m).to_broadcast([P, NT, nb, m])
                    place(l, o, k, s)
                o = att[:, d, :].rearrange("p (t u) -> p t u", t=NT)
                s = ax_ps[:, 2, :].rearrange("p (t u) -> p t u", t=NT)
                k = m_base[:, d, :].bitcast(U32).rearrange("p (a u) -> p a u", a=1).to_broadcast([P, NT, CHUNK])
                place(len(LEVELS), o, k, s)

            def states(h, d):
                dve.wait_ge(upd_done, 2 * h + (d + 1))
                if not isinstance(h, int):
                    dve.wait_ge(o_done, h)
                for n in range(3):
                    u = ax_ps[:, 4, n * P:(n + 1) * P]
                    if n == 0:
                        nc.vector.tensor_copy(state[:, d, 0, :], u).then_inc(state_ready, 1)
                    else:
                        dve.wait_ge(state_ready, 6 * h + (3 * d + n))
                        ch = FEED[d][n]
                        STT(state[:, d, n, :], state[:, d, n - 1, :], tot[:, d, ch:ch + 1], u,
                            ALU.mult, ALU.add).then_inc(state_ready, 1)

            def normalise(h, m):
                dve.wait_ge(root_ready, 3 * h + (m + 1))
                nc.vector.reciprocal(rms[:, :], rms[:, :]).then_inc(rinv_ready, 1)
                dve.wait_ge(rinv_ready, 3 * h + (m + 1))
                v = (n_q, n_k, z_a)[m][:, :]
                TT(v, v, rms[:, :], ALU.mult).then_inc(normed, 1)

            def tile(h, j):
                ps = mm_ps[:, j % 3, :]
                dve.wait_ge(unit_done, NU * h + (2 * j + 2))
                dve.wait_ge(tile_act, 9 * h + (j + 1))
                if j in (NQ, NK):
                    if not isinstance(h, int):
                        dve.wait_ge(s_done, 4 * h)
                    TS((n_q if j == NQ else n_k)[:, :], ps, cols[:, 1 + j - NQ:2 + j - NQ], None,
                       ALU.mult).then_inc(tile_dve, 1)
                else:
                    o = {HQ: qry, HG: gate, NG: n_gate}[j]
                    TT(o[:, :], ps, sig[:, :], ALU.mult).then_inc(tile_dve, 1)

            def late(i, g):
                if i == 0:
                    normalise(g, 2)
                    tile(g, NG)
                if 1 <= i <= 4:
                    t = i - 1
                    dve.wait_ge(s_done, 4 * g + (t + 1))
                    if t == 0:
                        dve.wait_ge(bias_ready, g + 1)
                    if t >= 2:
                        dve.wait_ge(pt_done, 4 * g + (t - 1))
                    off = (KH - 2 * t - 2) * GRID_W
                    STT(prob[:, t % 2, :], ax_ps[:, t % 2, :], SCALE, bias[:, off:off + S],
                        ALU.mult, ALU.add).then_inc(s_biased, 1)
                    dve.wait_ge(s_biased, 4 * g + (t + 1))
                    nc.vector.tensor_reduce(soft[:, 0, t:t + 1], prob[:, t % 2, :], AX.X, ALU.max).then_inc(s_max, 1)
                    dve.wait_ge(s_max, 4 * g + (t + 1))
                    TS(soft[:, 1, t:t + 1], soft[:, 0, t:t + 1], -1.0, None, ALU.mult).then_inc(s_neg, 1)
                if 2 <= i <= 5:
                    t = i - 2
                    dve.wait_ge(e_done, 4 * g + (t + 1))
                    nc.vector.reciprocal(soft[:, 3, t:t + 1], soft[:, 2, t:t + 1]).then_inc(e_recip, 1)
                    dve.wait_ge(e_recip, 4 * g + (t + 1))
                    TS(prob[:, t % 2, :], prob[:, t % 2, :], soft[:, 3, t:t + 1], None, ALU.mult).then_inc(p_ready, 1)
                if i == 7:
                    dve.wait_ge(pv_done, 4 * g + 4)
                    TT(z_b[:, :], ax_ps[:, 4, :], n_gate[:, :], ALU.mult).then_inc(zb_ready, 1)

            def head(h):
                us = Units(0, NU, h)
                for i in range(NU):
                    split_lo(dve, us, i + AHEAD)
                    if not isinstance(h, int):
                        late(i, h - 1)
                    if i == 2 and isinstance(h, int):
                        dve.wait_ge(pool_step, POOL_STEPS)
                        nc.vector.memset(att[:, :, :], 0.0).then_inc(att_zero, 1)
                        dve.wait_ge(att_zero, 1)
                    if i in (2, 10, 12, 14):
                        tile(h, i // 2 - 1)
                    if i == 3:
                        if isinstance(h, int):
                            dve.wait_ge(lb_step, 6)
                        else:
                            dve.wait_ge(key_ready, 2 * h)
                        TS(low_h[:, :], low[:, bass.ds(h, 1), :].rearrange("p a c -> p (a c)"), 1.0, None,
                           ALU.mult).then_inc(low_ready, 1)
                    if i in (4, 6):
                        forget_gate(h, i // 2 - 2)
                    if i == 9:
                        products(h, 0)
                    if i == 12:
                        products(h, 1)
                    if i in (5, 9):
                        chain(h, i // 9)
                    if i == 17 and not isinstance(h, int):
                        dve.wait_ge(zb_stored, 16 * h)
                    if i == 11:
                        states(h, 0)
                    if i == 14:
                        states(h, 1)
                        normalise(h, 0)
                    if i == 16:
                        dve.wait_ge(osq_ready, h + 1)
                        if not isinstance(h, int):
                            dve.wait_ge(za_stored, 16 * h)
                        STT(z_a[:, :], ax_ps[:, 4, :], cols[:, 0:1], gate[:, :], ALU.mult, ALU.mult).then_inc(za_part, 1)
                        normalise(h, 1)

            head(0)
            with dve.Fori(1, H) as h:
                head(h)

            def merge_y(n, slot, us, i):
                dve.wait_ge(gate_ready, 2 * n + 2)
                for b in range(2):
                    dve.wait_ge(unit_done, us.num(i + b) + 1)
                    TT(g_ab[:, slot, b, :], branch_ps(slot, b), g_ab[:, slot, b, :], ALU.mult).then_inc(y_part, 1)
                dve.wait_ge(y_part, 2 * n + 2)
                if not (isinstance(n, int) and n == 0):
                    dve.wait_ge(y_stored, 16 * n)
                TT(y_out[:, :], g_ab[:, slot, 0, :], g_ab[:, slot, 1, :], ALU.add).then_inc(y_ready, 1)

            def z_lo_tiles(k0, k1):
                for k in range(k0, k1):
                    dve.wait_ge(z_hi_done, k + 1)
                    TT(z_lo[k // H][:, k % H, :], back[:, k // 2 % 2, k % 2, :], z_hi[k // H][:, k % H, :].bitcast(F32),
                       ALU.subtract).then_inc(z_lo_done, 1)

            us = Units(U_MERGE)
            for i in range(8):
                split_lo(dve, us, i + AHEAD)
                late(i, H - 1)
                if i:
                    z_lo_tiles(i if i > 1 else 0, i + 1)

            def merge_pair(r, is_first=False):
                us = Units(U_MERGE + 8, 12, r)
                for i in range(12):
                    split_lo(dve, us, i + AHEAD)
                    if is_first and i == 0:
                        z_lo_tiles(H, 2 * H)
                    if i in (2, 8):
                        merge_y(r * 2 + i // 8, i // 8, us, i - 2)

            merge_pair(0, is_first=True)
            with dve.Fori(1, KT // 2 - 1) as r:
                merge_pair(r)

            def act_lo_tiles(k0, k1, phase):
                for k in range(k0, k1):
                    n = phase * (KT // 2) + k // 2
                    dve.wait_ge(a_hi_done, phase * KT + k + 1)
                    TT(act_lo[:, k, :], back[:, n % 2, k % 2, :], act_hi[:, k, :].bitcast(F32),
                       ALU.subtract).then_inc(a_lo_done, 1)

            us = Units(U_OUT - 4)
            for i in range(4):
                split_lo(dve, us, i + AHEAD, 1024 if i < 2 else out_width(i - 2))
                if i == 2:
                    merge_y(KT - 2, 0, us, 0)
                act_lo_tiles(4 * i, min(4 * i + 4, 14), 0)
            merge_y(KT - 1, 1, us, 2)

            def running_sum(c):
                dve.wait_ge(x2_sq, 4 * c)
                dve.wait_ge(ss_sum, c)
                TT(stat[:, 3, :], stat[:, 3, :], ssq[:, :], ALU.add).then_inc(ss_sum, 1)

            def residual(c, us):
                dve.wait_ge(xg_in, 16 * c + 16)
                if not (isinstance(c, int) and c == 0):
                    dve.wait_ge(x2_stored, 16 * c)
                    dve.wait_ge(x2_turned, 4 * c)
                for t in range(NT):
                    acc_full(dve, us, c, t)
                    TT(x2g[:, t, :], acc(t), xg[:, t, :], ALU.add).then_inc(x2_ready, 1)

            def out_group(c, is_first=False):
                us = Units(U_OUT, 6, c)
                for i in range(6):
                    split_lo(dve, us, i + AHEAD, out_width(i + AHEAD))
                    if is_first and i == 1:
                        act_lo_tiles(14, KT, 0)
                    if is_first and i == 3:
                        for k in range(PT):
                            dve.wait_ge(p_hi_done, k + 1)
                            TT(p_lo[:, k, :], ax_ps[:, 1 + k, :], p_hi[:, k, :].bitcast(F32),
                               ALU.subtract).then_inc(p_lo_done, 1)
                    if not is_first and i == 1:
                        running_sum(c)
                residual(c, us)

            nc.vector.memset(stat[:, 3, :], 0.0).then_inc(ss_sum, 1)
            out_group(0, is_first=True)
            with dve.Fori(1, 4) as c:
                out_group(c)
            act_lo_tiles(0, 4, 1)
            running_sum(4)

            def ple_group(c, is_first=False, is_last=False):
                us = Units(U_PLE, 6, c)
                for i in range(6):
                    if not (is_last and i + AHEAD >= 6):
                        split_lo(dve, us, i + AHEAD, 1536)
                    if i == 1:
                        if not (isinstance(c, int) and c == 0):
                            dve.wait_ge(res_ready, 4 * c)
                        for t in range(NT):
                            dve.wait_ge(unit_done, us.num(1))
                            nc.vector.tensor_copy(p_w[:, t, :], ax_ps[:, 1 + t, :]).then_inc(pw_ready, 1)
                    if is_first and i == 2:
                        dve.wait_ge(rstd_root, 1)
                        nc.vector.reciprocal(stat[:, 2, :], stat[:, 1, :]).then_inc(rstd_ready, 1)
                    if is_first and i < 4:
                        act_lo_tiles(4 + 3 * i, 7 + 3 * i, 1)
                dve.wait_ge(x2_in, 16 * c + 16)
                dve.wait_ge(pw_ready, 4 * c + 4)
                if not (isinstance(c, int) and c == 0):
                    dve.wait_ge(out_stored, 64 * c)
                for t in range(NT):
                    dve.wait_ge(g_ready, 4 * c + (t + 1))
                    TT(p_w[:, t, :], p_w[:, t, :], g_sig[:, t, :], ALU.mult).then_inc(gp_ready, 1)
                    dve.wait_ge(gp_ready, 4 * c + (t + 1))
                    TT(res[:, t, :], p_w[:, t, :], xg[:, t, :], ALU.add).then_inc(res_ready, 1)

            ple_group(0, is_first=True)
            with dve.Fori(1, 3) as c:
                ple_group(c)
            ple_group(3, is_last=True)

        @block.tensor
        def _(pe):
            MM = nc.tensor.matmul

            def turn_h(k):
                if k >= 5:
                    pe.wait_ge(h_lo, k - 4)
                for t in range(NT):
                    mm = nc.tensor.transpose(ax_ps[:, k % 5, t * P:(t + 1) * P], x_in[:, t, k * P:(k + 1) * P], ident[:, :])
                mm.then_inc(h_turned, 1)

            def columns(us, i, bank, k0, kn, start, stop, m_hi, m_lo, first=False, split=None):
                pe.wait_ge(lo_done, us.num(i) + 1)
                s = us.slot(i)
                for k in range(kn):
                    if first:
                        if k0 + k + 4 < KT:
                            turn_h(k0 + k + 4)
                        pe.wait_ge(h_lo, k0 + k + 1)
                    if split is not None:
                        pe.wait_ge(z_lo_done, split + k + 1)
                    wh, wl = w_hi[:, s, k * P:(k + 1) * P], w_lo[:, s, k * P:(k + 1) * P]
                    MM(bank, wh, m_hi[:, k0 + k, :], start=start and k == 0, stop=False)
                    MM(bank, wh, m_lo[:, k0 + k, :], start=False, stop=False)
                    mm = MM(bank, wl, m_hi[:, k0 + k, :], start=False, stop=stop and k == kn - 1)
                mm.then_inc(unit_done, 1)

            def tile_free(h, j):
                if isinstance(h, int) and h == 0 and j < 3:
                    return
                pj = (j - 3) % 9
                pe.wait_ge(tile_act, 9 * h + (j - 2))
                if pj in DREAD:
                    pe.wait_ge(tile_dve, 5 * h + (DREAD[pj] - (5 if j < 3 else 0)))

            def intra(h, d):
                pe.wait_ge(q_side, 12 * h + (6 * d + 6))
                pe.wait_ge(k_side, 12 * h + (6 * d + 6))
                if d:
                    pe.wait_ge(att_ready, 2 * h + 1)
                    pe.wait_ge(val_ready, 2 * h + 1)
                elif not isinstance(h, int):
                    pe.wait_ge(s_biased, 4 * h)
                    pe.wait_ge(pt_ready, 4 * h)
                for l, m in enumerate(LEVELS):
                    for t in range(NT):
                        w = lev[:, l, t * P:(t + 1) * P]
                        o = (l % 2) * 256 + t * 64
                        MM(ax_ps[:, l // 2, o:o + 64], w, halves(w, m, d, "q"), start=True, stop=True)
                for t in range(NT):
                    c = slice(t * P, (t + 1) * P)
                    MM(ax_ps[:, 2, c], base_k[:, c], base_q[:, c], start=True, stop=True)
                for n, ch in enumerate(FEED[d]):
                    mm = nc.tensor.transpose(ax_ps[:, 3, n * P:(n + 1) * P], st_k[:, ch * P:(ch + 1) * P], ident[:, :])
                mm.then_inc(intra_done, 1)

            def updates(h, d):
                pe.wait_ge(kt_ready, 2 * h + (d + 1))
                if d:
                    pe.wait_ge(state_ready, 6 * h + 3)
                else:
                    pe.wait_ge(val_ready, 2 * h + 1)
                    if not isinstance(h, int):
                        pe.wait_ge(zb_ready, h)
                for n, ch in enumerate(FEED[d]):
                    mm = MM(ax_ps[:, 4, n * P:(n + 1) * P], st_kt[:, n * P:(n + 1) * P], val[:, ch * P:(ch + 1) * P],
                            start=True, stop=True)
                mm.then_inc(upd_done, 1)

            def outputs(h):
                pe.wait_ge(att_ready, 2 * h + 2)
                pe.wait_ge(state_ready, 6 * h + 6)
                for t in range(NT):
                    c = slice(t * P, (t + 1) * P)
                    terms = [(val[:, c], att[:, d, c]) for d in range(2)]
                    if t > 0:
                        terms.append((state[:, 0, t - 1, :], st_q[:, 0, c]))
                    if t < NT - 1:
                        terms.append((state[:, 1, NT - 2 - t, :], st_q[:, 1, c]))
                    for n, (lhs, rhs) in enumerate(terms):
                        mm = MM(ax_ps[:, 4, c], lhs, rhs, start=n == 0, stop=n == len(terms) - 1)
                mm.then_inc(o_done, 1)

            def mean_square(m):
                MM(ax_ps[:, m, :], mean_w[:, :], sqr[:, :], start=True, stop=True).then_inc(ms_done, 1)

            def turn_v():
                for t in range(NT):
                    c = slice(t * P, (t + 1) * P)
                    mm = nc.tensor.transpose(ax_ps[:, 3, c], v_t[:, c], ident[:, :])
                mm.then_inc(vt_done, 1)

            def late(i, g):
                if i < 4:
                    if i == 0:
                        pe.wait_ge(normed, 3 * g + 2)
                        pe.wait_ge(root_ready, 3 * g + 2)
                    if i >= 2:
                        pe.wait_ge(s_biased, 4 * g + (i - 1))
                    MM(ax_ps[:, i % 2, :], n_q[:, i * P:(i + 1) * P], n_k[:, :], start=True, stop=True).then_inc(s_done, 1)
                if 2 <= i <= 5:
                    t = i - 2
                    pe.wait_ge(p_ready, 4 * g + (t + 1))
                    if t == 0:
                        pe.wait_ge(root_ready, 3 * g + 3)
                        pe.wait_ge(val_ready, 2 * g + 2)
                    if t >= 2:
                        pe.wait_ge(pt_ready, 4 * g + (t - 1))
                    for k in range(NT):
                        c = slice(k * P, (k + 1) * P)
                        mm = nc.tensor.transpose(ax_ps[:, 2 + t % 2, c], prob[:, t % 2, c], ident[:, :])
                    mm.then_inc(pt_done, 1)
                if 3 <= i <= 6:
                    t = i - 3
                    pe.wait_ge(pt_ready, 4 * g + (t + 1))
                    if t == 0:
                        pe.wait_ge(za_part, g + 1)
                        pe.wait_ge(osq_ready, g + 1)
                    for k in range(NT):
                        c = slice(k * P, (k + 1) * P)
                        mm = MM(ax_ps[:, 4, t * P:(t + 1) * P], n_v[:, c], prob_t[:, t % 2, c],
                                start=k == 0, stop=k == NT - 1)
                    mm.then_inc(pv_done, 1)

            def head(h):
                us = Units(0, NU, h)
                for i in range(NU):
                    j = i // 2
                    if i % 2 == 0:
                        tile_free(h, j)
                    columns(us, i, mm_ps[:, j % 3, :], 8 * (i % 2), 8, i % 2 == 0, i % 2 == 1, act_hi, act_lo,
                            first=isinstance(h, int) and i < 2)
                    if not isinstance(h, int):
                        late(i, h - 1)
                    if i == 8:
                        intra(h, 0)
                    if i == 9:
                        pe.wait_ge(tile_act, 9 * h + (HI + 1))
                        pe.wait_ge(kt_ready, 2 * h + 1)
                        turn_v()
                    if i == 10:
                        updates(h, 0)
                    if i == 11:
                        intra(h, 1)
                    if i == 13:
                        updates(h, 1)
                        pe.wait_ge(tile_act, 9 * h + (NQ + 1))
                        pe.wait_ge(att_ready, 2 * h + 2)
                        mean_square(0)
                    if i == 15:
                        pe.wait_ge(tile_act, 9 * h + (NK + 1))
                        mean_square(1)
                        outputs(h)
                    if i == 17:
                        pe.wait_ge(osq_ready, h + 1)
                        mean_square(2)
                        pe.wait_ge(tile_act, 9 * h + (NV + 1))
                        pe.wait_ge(kt_ready, 2 * h + 2)
                        turn_v()

            pe.wait_ge(pool_step, 2)
            pe.wait_ge(pool_ready, 1)
            pe.wait_ge(x_normed, NT)
            for k in range(4):
                turn_h(k)
            head(0)
            with pe.Fori(1, H) as h:
                head(h)

            def gates(us, i, n, after_heads=False):
                for b in range(2):
                    if after_heads:
                        tile_free(H - 1, 9 + b)
                    else:
                        pe.wait_ge(gate_ready, 2 * n + (b - 1))
                    for e in range(2):
                        columns(us, i + 2 * b + e, mm_ps[:, b, :], 8 * e, 8, e == 0, e == 1, act_hi, act_lo)
                        yield

            def run(steps, after=None):
                for k, _ in enumerate(steps):
                    if after:
                        after(k)

            us = Units(U_MERGE)
            run(gates(us, 0, 0, after_heads=True), lambda k: late(k, H - 1))
            run(gates(us, 4, 1), lambda k: late(4 + k, H - 1))

            def branch(us, i, n, slot):
                for b in range(2):
                    if isinstance(n, int) and n < 2:
                        pe.wait_ge(tile_dve, 5 * H)
                        pe.wait_ge(zb_ready, H)
                    elif b == 0:
                        pe.wait_ge(y_part, 2 * n - 2)
                    columns(us, i + b, branch_ps(slot, b), 0, H, True, True, z_hi[b], z_lo[b],
                            split=H * b if isinstance(n, int) and n == 0 else None)

            def merge_pair(r):
                us = Units(U_MERGE + 8, 12, r)
                for e in range(2):
                    branch(us, 6 * e, r * 2 + e, e)
                    run(gates(us, 6 * e + 2, r * 2 + (2 + e)))

            merge_pair(0)
            with pe.Fori(1, KT // 2 - 1) as r:
                merge_pair(r)
            us = Units(U_OUT - 4)
            branch(us, 0, KT - 2, 0)
            branch(us, 2, KT - 1, 1)

            def rows(us, i, terms, last):
                pe.wait_ge(lo_done, us.num(i) + 1)
                s = us.slot(i)
                for t in range(NT):
                    for (w, a_h, a_l, o, start, stop) in terms(t):
                        wh, wl = w_hi[:, s, w * 512:(w + 1) * 512], w_lo[:, s, w * 512:(w + 1) * 512]
                        MM(o, a_h, wh, start=start, stop=False)
                        MM(o, a_l, wh, start=False, stop=False)
                        mm = MM(o, a_h, wl, start=False, stop=stop)
                    if last is not None and t < NT - 1:
                        mm.then_inc(last, 1)
                mm.then_inc(unit_done, 1)

            def turn_x2(c):
                pe.wait_ge(x2_ready, 4 * c + 4)
                pe.wait_ge(p_lo_done, PT)
                for f in range(4):
                    for t in range(NT):
                        mm = nc.tensor.transpose(ax_ps[:, 1 + f, t * P:(t + 1) * P], x2g[:, t, f * P:(f + 1) * P], ident[:, :])
                    mm.then_inc(x2_turned, 1)

            def out_group(c, is_first=False):
                us = Units(U_OUT, 6, c)
                for i, kn in enumerate(OUT_KT):
                    k0 = sum(OUT_KT[:i])
                    if i == 0 and is_first:
                        pe.wait_ge(gate_ready, 2 * KT)
                        pe.wait_ge(y_part, 2 * (KT - 1))

                    def terms(t):
                        if i == 0 and not is_first:
                            pe.wait_ge(x2_ready, 4 * c + (t - 3))
                        for k in range(kn):
                            if is_first and t == 0:
                                pe.wait_ge(a_lo_done, k0 + k + 1)
                            a = (k0 + k, slice(t * P, (t + 1) * P))
                            yield k, act_hi[:, a[0], a[1]], act_lo[:, a[0], a[1]], acc(t), k0 + k == 0, k0 + k == KT - 1

                    rows(us, i, terms, acc_done if i == 5 else None)
                    if i == 2 and is_first:
                        pe.wait_ge(p_landed, 16)
                        pe.wait_ge(y_part, 2 * KT)
                        for k in range(PT):
                            for t in range(NT):
                                mm = nc.tensor.transpose(ax_ps[:, 1 + k, t * P:(t + 1) * P], p_in[:, t, k * P:(k + 1) * P], ident[:, :])
                            mm.then_inc(p_turned, 1)
                    if i == 0 and not is_first:
                        turn_x2(c - 1)

            out_group(0, is_first=True)
            with pe.Fori(1, 4) as c:
                out_group(c)

            def ple_group(c, is_first=False):
                us = Units(U_PLE, 6, c)
                for i in range(6):
                    def terms(t):
                        tok = slice(t * P, (t + 1) * P)
                        if i == 0 and not is_first:
                            pe.wait_ge(pw_ready, 4 * c + (t - 3))
                            pe.wait_ge(g_ready, 4 * c + (t - 3))
                        if i == 0:
                            for k in range(PT):
                                yield k, p_hi[:, k, tok], p_lo[:, k, tok], ax_ps[:, 1 + t, :], k == 0, k == PT - 1
                            if is_first:
                                pe.wait_ge(x2_ready, 13 + t)
                        for k in ([0] if i == 0 else range(3 * i - 2, 3 * i + 1)):
                            if is_first and t == 0:
                                pe.wait_ge(a_lo_done, KT + k + 1)
                            w = PT if i == 0 else k - (3 * i - 2)
                            yield w, act_hi[:, k, tok], act_lo[:, k, tok], acc(t), k == 0, k == KT - 1

                    rows(us, i, terms, acc_done if i == 5 else None)
                    if is_first and i == 1:
                        pe.wait_ge(pw_ready, 4)
                        turn_x2(3)

            ple_group(0, is_first=True)
            with pe.Fori(1, 4) as c:
                ple_group(c)


INPUTS = ["x", "p", "norm_g", "w_in", "hgrn_lb", "hgrn_onorm", "na_qnorm", "na_knorm", "na_rpb",
          "w_branch_a", "w_branch_b", "w_out", "ple_norm", "w_ple_gate", "w_ple"]


def kernel(**inputs):
    import numpy as np
    import concourse.bacc as bacc
    from concourse.bass_utils import run_bass_kernel_spmd

    nc = bacc.Bacc("TRN2", target_bir_lowering=False, num_devices=1)
    arrays, args = {}, []
    for name in INPUTS:
        a = np.ascontiguousarray(inputs[name])
        arrays[f"in_{name}"] = a
        args.append(nc.dram_tensor(f"in_{name}", a.shape, mybir.dt.from_np(a.dtype), kind="ExternalInput").ap())
    shape = np.asarray(inputs["x"]).shape
    args.append(nc.dram_tensor("out_0", shape, F32, kind="ExternalOutput").ap())
    build_kernel(nc, *args)
    r = run_bass_kernel_spmd(nc, [arrays], core_ids=[0])
    return r.results[0]["out_0"]
```

```python
from contextlib import ExitStack

import concourse.bass as bass
from concourse import mybir

ALU = mybir.AluOpType
ACT = mybir.ActivationFunctionType
F32 = mybir.dt.float32
F32R = mybir.dt.float32r
U32 = mybir.dt.uint32
AX = mybir.AxisListType

P = 128
RING = 3
AHEAD = 2
GRID_W, KH, KW = 64, 8, 16
CHUNK = 128
LEVELS = (64, 32, 16, 8)
BASE = 8
NL = len(LEVELS) + 2
EPS, F_MIN, NEG = 1e-6, 1e-6, -1e30
HQ, HF, HB, HI, HG, NQ, NK, NV, NG = range(9)


def build_kernel(nc, x, p, norm_g, w_in, hgrn_lb, hgrn_onorm, na_qnorm, na_knorm, na_rpb,
                 w_branch_a, w_branch_b, w_out, ple_norm, w_ple_gate, w_ple, out):
    S, D = x.shape[1], x.shape[2]
    HW = w_branch_a.shape[1]
    H = HW // P
    PLE = p.shape[3]
    NT, KT, PT = S // P, D // P, PLE // P
    NR, NC = 2 * KH - 1, 2 * KW - 1
    ROWS = S // GRID_W
    assert S == 512 and D == 2048 and H == 8 and ROWS == KH and PT == 2
    SCALE = float(P) ** -0.5
    QC, KC = GRID_W // NT, 2 * KW
    KEY_COL = [min(max(QC * t - KW // 2, 0), GRID_W - KC) for t in range(NT)]
    V_COL = sorted({c + b * (KC // 2) for c in KEY_COL for b in range(2)})
    KIND = [0, 1, 1, 2]
    PITCH = 2 * KC
    COL = [0, 2 * HW, 3 * HW, HW, 4 * HW, 5 * HW, 6 * HW, 7 * HW, 8 * HW]
    MA, MB = 9 * HW, 9 * HW + D
    NU = 18
    U_MERGE = H * NU
    U_OUT = U_MERGE + 6 * KT
    U_PLE = U_OUT + 6 * 4
    U_END = U_PLE + 6 * 4
    OUT_KT = [3, 3, 3, 3, 2, 2]
    DREAD = {HQ: 1, HG: 2, NQ: 3, NK: 4, NG: 5}

    x_v = x[0].rearrange("(t p) d -> p t d", p=P)
    out_v = out[0].rearrange("(t p) d -> p t d", p=P)
    p_v = p[0, 0].rearrange("(t p) e -> p t e", p=P)
    win_v = w_in[0].rearrange("(k p) n -> p k n", p=P)
    wa_v = w_branch_a[0].rearrange("(k p) n -> p k n", p=P)
    wb_v = w_branch_b[0].rearrange("(k p) n -> p k n", p=P)
    wo_v = w_out[0].rearrange("(k p) n -> p k n", p=P)
    wg_v = w_ple_gate[0].rearrange("(k p) n -> p k n", p=P)
    wp_v = w_ple[0].rearrange("(k p) n -> p k n", p=P)
    pn_v = ple_norm[0].rearrange("(c f p) -> c p f", p=P, f=4)

    z_dram = nc.dram_tensor("z_dram", [2 * H, P, S], F32, kind="Internal").ap()
    y_dram = nc.dram_tensor("y_dram", [KT, P, S], F32, kind="Internal").ap()
    x2_dram = nc.dram_tensor("x2_dram", [4, P, NT * 512], F32, kind="Internal").ap()
    x2t_dram = nc.dram_tensor("x2t_dram", [KT, P, S], F32, kind="Internal").ap()
    rpb_dram = nc.dram_tensor("rpb_dram", [H, QC * NR * PITCH], F32, kind="Internal").ap()

    with ExitStack() as ctx:
        ctx.enter_context(nc.allow_non_contiguous_dma(reason="norm weights, one element per partition"))

        def sb(name, shape, dt=F32, where=ctx):
            return where.enter_context(nc.sbuf_tensor(name, shape, dt))

        def sem(name):
            return ctx.enter_context(nc.semaphore(name))

        act_hi = sb("act_hi", [P, KT, S], F32R)
        act_lo = sb("act_lo", [P, KT, S], F32R)
        w_raw = sb("w_raw", [P, RING, 1536])
        w_hi = sb("w_hi", [P, RING, 1536], F32R)
        w_lo = sb("w_lo", [P, RING, 1536], F32R)
        ident = sb("ident", [P, P])
        mean_w = sb("mean_w", [P, P], F32R)
        cols = sb("cols", [P, 4])
        norm_c = sb("norm_c", [P, KT])
        eps_c = sb("eps_c", [P, 1])
        stat = sb("stat", [P, 4, NT])
        low = sb("low", [P, H, 4])
        low_h = sb("low_h", [P, 4])
        reset = sb("reset", [P, S])
        m_lev = sb("m_lev", [P, len(LEVELS), CHUNK])
        m_base = sb("m_base", [P, 2, CHUNK])
        m_win = sb("m_win", [P, 3, KC])
        rpb_pad = sb("rpb_pad", [P, PITCH])
        mm_ps = ctx.enter_context(nc.psum_tensor("mm_ps", [P, 3, 512], F32))
        ax_ps = ctx.enter_context(nc.psum_tensor("ax_ps", [P, 5, 512], F32))

        with ExitStack() as first:
            x_in = sb("x_in", [P, NT, D], where=first)
            x_sq = sb("x_sq", [P, D], where=first)
            lb_col = sb("lb_col", [P, 4, 2 * H], where=first)
            mean_in = sb("mean_in", [P, P], where=first)
        with ExitStack() as heads:
            logf = sb("logf", [P, S], where=heads)
            key = sb("key", [P, 2, S], where=heads)
            qry = sb("qry", [P, S], where=heads)
            cum = sb("cum", [P, S], where=heads)
            with ExitStack() as decay:
                dif = sb("dif", [P, 2, S], where=decay)
            squares = sb("squares", [P, 2, S], F32R, where=heads)
            lev_q = sb("lev_q", [P, len(LEVELS), S], where=heads)
            lev_k = sb("lev_k", [P, len(LEVELS), S], where=heads)
            base_q = sb("base_q", [P, S], where=heads)
            base_k = sb("base_k", [P, S], where=heads)
            st_q = sb("st_q", [P, 2, S], where=heads)
            st_k = sb("st_k", [P, S], where=heads)
            st_kt = sb("st_kt", [P, 3 * P], where=heads)
            tot = sb("tot", [P, 2, NT], where=heads)
            state = sb("state", [P, 2, 3, P], where=heads)
            att = sb("att", [P, 2, S], where=heads)
            att_sum = base_k
            val = sb("val", [P, S], where=heads)
            gate = sb("gate", [P, S], where=heads)
            z_a = sb("z_a", [P, S], where=heads)
            v_t = sb("v_t", [P, S], where=heads)
            temp = sb("temp", [P, S], where=heads)
            rms = sb("rms", [P, S], where=heads)
            n_q = sb("n_q", [P, S], where=heads)
            n_k = sb("n_k", [P, S], where=heads)
            n_v = sb("n_v", [P, len(V_COL), P], where=heads)
            n_gate = sb("n_gate", [P, S], where=heads)
            bias = sb("bias", [P, KH, PITCH], where=heads)
            bias_w = sb("bias_w", [P, 3, KC, KH], where=heads)
            prob = sb("prob", [P, 2, KH * KC], where=heads)
            prob_t = sb("prob_t", [P, 2, KH * KC], where=heads)
            soft = sb("soft", [P, 4, NT], where=heads)
            z_b = sb("z_b", [P, S], where=heads)
        with ExitStack() as merge:
            g_ab = sb("g_ab", [P, 2, 2, S], where=merge)
            za_hi = sb("za_hi", [P, H, S], F32R, where=merge)
            za_lo = sb("za_lo", [P, H, S], F32R, where=merge)
            back = sb("back", [P, 2, 2, S], where=merge)
            zb_hi = sb("zb_hi", [P, H, S], F32R, where=merge)
            zb_lo = sb("zb_lo", [P, H, S], F32R, where=merge)
            y_out = sb("y_out", [P, S], where=merge)
            z_hi, z_lo = (za_hi, zb_hi), (za_lo, zb_lo)
        with ExitStack() as last:
            p_in = sb("p_in", [P, NT, PLE], where=last)
            p_hi = sb("p_hi", [P, PT, S], F32R, where=last)
            p_lo = sb("p_lo", [P, PT, S], F32R, where=last)
            xg = sb("xg", [P, NT, 512], where=last)
            x2g = sb("x2g", [P, NT, 512], where=last)
            x2t = sb("x2t", [P, 4, S], where=last)
            sb("below_back", [P, 1024], where=last)
            sb("under_back", [P, 2 * 2 * S], where=last)
            junk = sb("junk", [P, 512], where=last)
            pn_c = sb("pn_c", [P, 4], where=last)
            ssq = sb("ssq", [P, NT], where=last)
            p_w = sb("p_w", [P, NT, 512], where=last)
            g_sig = sb("g_sig", [P, NT, 512], where=last)
            res = sb("res", [P, NT, 512], where=last)

        raw_ready = [sem(f"raw_ready{s}") for s in range(RING)]
        pw_raw = sem("pw_raw")
        hi_done, lo_done, unit_done, acc_done = (sem(n) for n in ("hi_done", "lo_done", "unit_done", "acc_done"))
        x_ready = [sem(f"x_ready{t}") for t in range(NT)]
        const_in, lb_in, rpb_in, rpb_out = (sem(n) for n in ("const_in", "lb_in", "rpb_in", "rpb_out"))
        pool_step, pool_ready, mean_ready, lb_step, eps_ready = (
            sem(n) for n in ("pool_step", "pool_ready", "mean_ready", "lb_step", "eps_ready"))
        x_tail = sem("x_tail")
        x_sumsq, x_root, x_recip, x_normed = (sem(n) for n in ("x_sumsq", "x_root", "x_recip", "x_normed"))
        h_turned, h_hi, h_lo = (sem(n) for n in ("h_turned", "h_hi", "h_lo"))
        tile_act, tile_dve, low_ready, att_zero = (sem(n) for n in ("tile_act", "tile_dve", "low_ready", "att_zero"))
        base_part, lev_done = sem("base_part"), sem("lev_done")
        att_part = [sem(f"att_part{l}") for l in range(len(LEVELS))]
        forget, key_ready, log_ready, cum_ready = (sem(n) for n in ("forget", "key_ready", "log_ready", "cum_ready"))
        dif_ready, dec_ready, q_side, k_side = (sem(n) for n in ("dif_ready", "dec_ready", "q_side", "k_side"))
        intra_done, att_ready, kt_ready = (sem(n) for n in ("intra_done", "att_ready", "kt_ready"))
        upd_done, state_ready, o_done, osq_ready = (sem(n) for n in ("upd_done", "state_ready", "o_done", "osq_ready"))
        sq_hi_done, sq_lo_done = sem("sq_hi_done"), sem("sq_lo_done")
        ms_done, root_ready, rinv_ready, normed = (sem(n) for n in ("ms_done", "root_ready", "rinv_ready", "normed"))
        za_last, zb_last, x2_last, x2t_last = (sem(n) for n in ("za_last", "zb_last", "x2_last", "x2t_last"))
        vt_done, val_ready = sem("vt_done"), sem("val_ready")
        za_part, za_stored, zb_ready, zb_stored = (sem(n) for n in ("za_part", "za_stored", "zb_ready", "zb_stored"))
        bias_in, bias_ready = sem("bias_in"), sem("bias_ready")
        s_done, s_biased, s_max, s_neg = (sem(n) for n in ("s_done", "s_biased", "s_max", "s_neg"))
        e_done, e_recip, p_ready = (sem(n) for n in ("e_done", "e_recip", "p_ready"))
        pt_done, pt_ready, pv_done = (sem(n) for n in ("pt_done", "pt_ready", "pv_done"))
        z_in = [sem("z_in0"), sem("z_in1")]
        z_hi_done, z_lo_done, gate_ready = (sem(n) for n in ("z_hi_done", "z_lo_done", "gate_ready"))
        y_part, y_ready, y_stored = (sem(n) for n in ("y_part", "y_ready", "y_stored"))
        a_in = [sem("a_in0"), sem("a_in1")]
        a_hi_done, a_lo_done = sem("a_hi_done"), sem("a_lo_done")
        p_landed, p_turned, p_hi_done, p_lo_done = (sem(n) for n in ("p_landed", "p_turned", "p_hi_done", "p_lo_done"))
        xg_in, pn_in, x2_ready, x2_sq, ss_sum = (sem(n) for n in ("xg_in", "pn_in", "x2_ready", "x2_sq", "ss_sum"))
        x2_turned, x2t_ready, x2_stored, x2t_stored = (
            sem(n) for n in ("x2_turned", "x2t_ready", "x2_stored", "x2t_stored"))
        rstd_root, rstd_ready, pw_ready, x2_in = (sem(n) for n in ("rstd_root", "rstd_ready", "pw_ready", "x2_in"))
        g_ready, gp_ready, res_ready, out_stored = (sem(n) for n in ("g_ready", "gp_ready", "res_ready", "out_stored"))

        ORDER = (len(LEVELS), NL - 1, *range(len(LEVELS)))
        MS_BANK = (2, 0, 1)
        POOL_STEPS = 20 + 3 * (len(LEVELS) - 1)

        block = ctx.enter_context(nc.Block())

        class Units:

            def __init__(self, first, step=0, r=0):
                self.first, self.step, self.r = first, step, r

            def num(self, i):
                return self.r * self.step + (self.first + i)

            def slot(self, i):
                return (self.first + i) % RING

            def fills(self, i):
                return self.r * (self.step // RING) + ((self.first + i) // RING + 1)

            def reuses(self, i):
                return not (isinstance(self.r, int) and self.num(i) < RING)

        def load_w(sp, us, i, src):
            if us.reuses(i):
                sp.wait_ge(lo_done, us.num(i) - (RING - 1))
            k, n = src.shape[1], src.shape[2]
            dst = w_raw[:, us.slot(i), 0:k * n].rearrange("p (k n) -> p k n", k=k)
            sp.dma_start(dst, src).then_inc(raw_ready[us.slot(i)], 16)

        def split_hi(act, us, i, width=1024):
            s = us.slot(i)
            act.wait_ge(raw_ready[s], us.fills(i) * 16)
            if us.reuses(i):
                act.wait_ge(unit_done, us.num(i) - (RING - 1))
            nc.scalar.activation(w_hi[:, s, 0:width], w_raw[:, s, 0:width], ACT.Copy).then_inc(hi_done, 1)

        def split_lo(dve, us, i, width=1024):
            s = us.slot(i)
            dve.wait_ge(hi_done, us.num(i) + 1)
            if us.reuses(i):
                dve.wait_ge(unit_done, us.num(i) - (RING - 1))
            nc.vector.tensor_tensor(w_lo[:, s, 0:width], w_raw[:, s, 0:width],
                                    w_hi[:, s, 0:width].bitcast(F32), ALU.subtract).then_inc(lo_done, 1)

        def out_width(i):
            return OUT_KT[i % 6] * 512

        def halves(ap, m, d, side):
            h = int((side == "q") == (d == 0))
            return ap.rearrange("p (b h u) -> p b h u", h=2, u=m)[:, :, h, :]

        def reference(ap, l, d):
            if l < len(LEVELS):
                w, r = 2 * LEVELS[l], LEVELS[l] - 1 + d
            elif l == len(LEVELS):
                w, r = BASE, BASE // 2 - 1 + d
            else:
                w, r = CHUNK, (CHUNK - 1) * (1 - d)
            v = ap.rearrange("p (b w) -> p b w", w=w)
            return v, v[:, :, r:r + 1].to_broadcast([P, S // w, w]), w

        ST = [dict(q=slice(CHUNK, S), k=slice(0, S - CHUNK)), dict(q=slice(0, S - CHUNK), k=slice(CHUNK, S))]
        FEED = [[0, 1, 2], [3, 2, 1]]

        def rpb_rows(h):
            v = rpb_dram[bass.ds(h, 1), QC - 1:QC * NR * PITCH]
            return bass.AP(tensor=v.tensor, offset=v.offset, ap=[[NR * PITCH - 1, QC], [PITCH, KH], [1, KH * PITCH]])

        def by_column(ap):
            return ap.rearrange("p (r c) -> p c r", c=GRID_W)

        def columns_of(ap):
            return ap.rearrange("p (c r) -> p c r", r=ROWS)

        def queries_of(ap):
            return columns_of(ap)[:, :, ::-1]

        def key_window(t):
            return slice(KEY_COL[t] * ROWS, (KEY_COL[t] + KC) * ROWS)

        def acc(t):
            return mm_ps[:, t, :] if t < 3 else ax_ps[:, 0, :]

        def acc_full(eng, us, g, t):
            if t < NT - 1:
                eng.wait_ge(acc_done, g * (NT - 1) + (t + 1))
            else:
                eng.wait_ge(unit_done, us.num(6))

        def branch_ps(slot, b):
            return mm_ps[:, 2, :] if slot == 0 and b == 0 else ax_ps[:, 0 if slot == 0 else 1 + b, :]

        @block.sync
        def _(sp):
            us = Units(0)
            for t in range(NT):
                if t == NT - 1:
                    load_w(sp, us, 0, win_v[:, 0:8, COL[HQ]:COL[HQ] + P])
                sp.dma_start(x_in[:, t, :], x_v[:, t, :]).then_inc(x_ready[t], 16)
            load_w(sp, us, 1, win_v[:, 8:16, COL[HQ]:COL[HQ] + P])

            def head(h):
                us = Units(0, NU, h)
                for i in range(NU):
                    if isinstance(h, int) and i < 2:
                        continue
                    load_w(sp, us, i, win_v[:, 8 * (i % 2):8 * (i % 2) + 8, bass.ds(h * P + COL[i // 2], P)])
                    if i == 7 and not isinstance(h, int):
                        sp.wait_ge(normed, 3 * h)
                        sp.dma_start(z_dram[bass.ds(h - 1, 1)].rearrange("a p s -> p (a s)"), z_a[:, :]).then_inc(za_stored, 16)
                    if i == 10:
                        if isinstance(h, int):
                            sp.wait_ge(rpb_out, 16 * H)
                        else:
                            sp.wait_ge(bias_ready, 3 * h)
                        sp.dma_start(bias[:, :, :].rearrange("p r x -> p (r x)"), rpb_rows(h)).then_inc(bias_in, 16)
                    if i == 13 and not isinstance(h, int):
                        sp.wait_ge(zb_ready, h)
                        sp.dma_start(z_dram[bass.ds(h + (H - 1), 1)].rearrange("a p s -> p (a s)"), z_b[:, :]).then_inc(zb_stored, 16)

            head(0)
            with sp.Fori(1, H) as h:
                head(h)

            us = Units(U_MERGE)
            for i in range(8):
                c = (MA if i % 4 < 2 else MB) + P * (i // 4)
                load_w(sp, us, i, win_v[:, 8 * (i % 2):8 * (i % 2) + 8, c:c + P])

            def branches(us, i, n):
                load_w(sp, us, i, wa_v[:, :, bass.ds(n * P, P)])
                load_w(sp, us, i + 1, wb_v[:, :, bass.ds(n * P, P)])

            def store_y(n):
                sp.wait_ge(y_ready, n + 1)
                sp.dma_start(y_dram[bass.ds(n, 1)].rearrange("a p s -> p (a s)"), y_out[:, :]).then_inc(y_stored, 16)

            def merge_pair(r, is_first=False):
                us = Units(U_MERGE + 8, 12, r)
                for e in range(2):
                    branches(us, 6 * e, r * 2 + e)
                    for i in range(4):
                        load_w(sp, us, 6 * e + 2 + i, win_v[:, 8 * (i % 2):8 * (i % 2) + 8,
                               bass.ds(r * (2 * P) + ((MA if i < 2 else MB) + (2 + e) * P), P)])
                        if i == 0 and not (is_first and e == 0):
                            store_y(r * 2 + (e - 1))

            merge_pair(0, is_first=True)
            with sp.Fori(1, KT // 2 - 1) as r:
                merge_pair(r)
            us = Units(U_OUT - 4)
            branches(us, 0, KT - 2)
            store_y(KT - 3)
            branches(us, 2, KT - 1)

            def out_group(c, is_first=False):
                us = Units(U_OUT, 6, c)
                for i, kn in enumerate(OUT_KT):
                    k = sum(OUT_KT[:i])
                    load_w(sp, us, i, wo_v[:, k:k + kn, bass.ds(c * 512, 512)])
                    if is_first and i == 1:
                        store_y(KT - 2)
                    if is_first and i == 3:
                        store_y(KT - 1)
                if not is_first:
                    sp.wait_ge(x2_ready, 4 * c)
                    sp.dma_start(x2_dram[bass.ds(c - 1, 1)].rearrange("a p s -> p (a s)"),
                                 x2g[:, :, :].rearrange("p t j -> p (t j)")).then_inc(x2_stored, 16)
                    sp.wait_ge(x2t_ready, 4 * c)
                    sp.dma_start(x2t_dram[bass.ds(4 * c - 4, 4)].rearrange("f p s -> p f s"),
                                 x2t[:, :, :]).then_inc(x2t_stored, 16)
                sp.dma_start(xg[:, :, :], x_v[:, :, bass.ds(c * 512, 512)]).then_inc(xg_in, 16)
                sp.dma_start(pn_c[:, :], pn_v[bass.ds(c, 1)].rearrange("c p f -> p (c f)")).then_inc(pn_in, 16)

            out_group(0, is_first=True)
            with sp.Fori(1, 4) as c:
                out_group(c)

            def ple_unit(us, i, c):
                if i == 0:
                    sp.wait_ge(lo_done, us.num(0) - (RING - 1))
                    dst = w_raw[:, us.slot(0), 0:PT * 512].rearrange("p (k n) -> p k n", k=PT)
                    sp.dma_start(dst, wp_v[:, :, bass.ds(c * 512, 512)]).then_inc(pw_raw, 16)
                    dst = w_raw[:, us.slot(0), PT * 512:1536].rearrange("p (k n) -> p k n", k=1)
                    sp.dma_start(dst, wg_v[:, 0:1, bass.ds(c * 512, 512)]).then_inc(raw_ready[us.slot(0)], 16)
                else:
                    load_w(sp, us, i, wg_v[:, 3 * i - 2:3 * i + 1, bass.ds(c * 512, 512)])

            def store_out(c):
                for t in range(NT):
                    sp.wait_ge(res_ready, 4 * c + (t + 1))
                    sp.dma_start(out_v[:, t, bass.ds(c * 512, 512)], res[:, t, :]).then_inc(out_stored, 16)

            def ple_group(c, is_first=False):
                us = Units(U_PLE, 6, c)
                for i in range(6):
                    ple_unit(us, i, c)
                if is_first:
                    sp.wait_ge(x2_ready, 16)
                    sp.wait_ge(x2_stored, 16 * 3)
                    sp.wait_ge(x2_last, 16)
                else:
                    store_out(c - 1)
                sp.dma_start(xg[:, :, :].rearrange("p t j -> p (t j)"),
                             x2_dram[bass.ds(c, 1)].rearrange("a p s -> p (a s)")).then_inc(x2_in, 16)

            ple_group(0, is_first=True)
            with sp.Fori(1, 4) as c:
                ple_group(c)
            store_out(3)
            sp.wait_ge(out_stored, 16 * 16)

        @block.gpsimd
        def _(pool):
            steps = [0]

            def link(ins):
                steps[0] += 1
                ins.then_inc(pool_step, 1)
                pool.wait_ge(pool_step, steps[0])

            def keep(v, pattern, base, cm, fill, compare=ALU.is_ge):
                link(nc.gpsimd.affine_select(out=v, in_=v, compare_op=compare, fill=fill, base=base,
                                             pattern=pattern, channel_multiplier=cm))

            link(nc.gpsimd.memset(ident[:, :], 0.0))
            keep(ident[:, :], [[-1, P]], 0, 1, 1.0, ALU.not_equal)
            nc.gpsimd.memset(mean_in[:, :], 1.0 / P).then_inc(pool_ready, 1)
            pool.dma_start(norm_c[:, :], norm_g[0].rearrange("(k p) -> p k", p=P)).then_inc(const_in, 16)
            pool.dma_start(cols[:, 0:1], hgrn_onorm.rearrange("a p -> p a")).then_inc(const_in, 16)
            pool.dma_start(cols[:, 1:2], na_qnorm.rearrange("a p -> p a")).then_inc(const_in, 16)
            pool.dma_start(cols[:, 2:3], na_knorm.rearrange("a p -> p a")).then_inc(const_in, 16)
            for d in range(2):
                pool.dma_start(lb_col[:, 0, d * H:(d + 1) * H],
                               hgrn_lb[0, d].rearrange("(h p) -> p h", p=P)).then_inc(lb_in, 16)
            link(nc.gpsimd.memset(rpb_pad[:, :], 0.0))
            pool.dma_start(rpb_pad[0:H * NR, KW:KW + NC],
                           na_rpb[0].rearrange("h r c -> (h r) c")).then_inc(rpb_in, 16)
            pool.wait_ge(rpb_in, 16)
            for h in range(H):
                src = rpb_pad[h * NR:(h + 1) * NR, :].rearrange("r (a x) -> r a x", a=1).to_broadcast([NR, QC, PITCH])
                dst = rpb_dram[h].rearrange("(c r x) -> r c x", c=QC, x=PITCH)
                pool.dma_start(dst, src).then_inc(rpb_out, 16)
            link(nc.gpsimd.memset(reset[:, :], 1.0))
            link(nc.gpsimd.memset(reset[:, :].rearrange("p (c u) -> p c u", u=CHUNK)[:, :, 0:1], 0.0))
            link(nc.gpsimd.memset(m_lev[:, :, :], 1.0))
            link(nc.gpsimd.memset(m_base[:, :, :], 1.0))
            blocks = [m_lev[:, l, :] for l in range(len(LEVELS))] + [m_base[:, 0, :]]
            for l in range(1, len(blocks)):
                w = LEVELS[l - 1]
                v = blocks[l].rearrange("p (b u) -> p b u", u=w)
                keep(v, [[-w, CHUNK // w], [0, w]], 0, 1, 0.0)
                keep(v, [[w, CHUNK // w], [0, w]], w - 1, -1, 0.0)
            for l in range(len(LEVELS)):
                ins = nc.gpsimd.tensor_tensor(blocks[l], blocks[l], blocks[l + 1], ALU.subtract)
                link(ins)
            for d in range(2):
                v = m_base[:, d, :].rearrange("p (b u) -> p b u", u=BASE)
                nb = CHUNK // BASE
                if d == 0:
                    keep(v, [[BASE, nb], [1, BASE]], 0, -1, 0.0)
                else:
                    keep(v, [[-BASE, nb], [-1, BASE]], 0, 1, 0.0)
                    keep(v, [[BASE, nb], [0, BASE]], BASE - 1, -1, 0.0)
            link(nc.gpsimd.memset(m_win[:, :, :], 0.0))
            half = KW // 2
            for kind, first, lower, upper in ((0, 0, slice(0, KC), slice(KW, KC)),
                                              (1, -half, slice(0, KC), slice(0, KC)),
                                              (2, -KW, slice(0, KW), slice(0, KC))):
                v = m_win[:, kind, lower]
                keep(v, [[KH, v.shape[1]]], KH * (first + lower.start + half + 1) - 1, -1, NEG)
                v = m_win[:, kind, upper]
                keep(v, [[-KH, v.shape[1]]], -KH * (first + upper.start - half + 1), 1, NEG)

            assert steps[0] == POOL_STEPS

            def key_scale(h, d):
                pool.wait_ge(tile_act, 9 * h + (HF + d + 1))
                pool.wait_ge(low_ready, h + 1)
                nc.gpsimd.tensor_tensor(key[:, d, :], key[:, d, :], low_h[:, 2 + d:3 + d].to_broadcast([P, S]),
                                        ALU.mult).then_inc(key_ready, 1)

            def key_sides(h, d):
                pool.wait_ge(key_ready, 2 * h + (d + 1))
                for n, l in enumerate(ORDER):
                    pool.wait_ge(dec_ready, 12 * h + (6 * d + n + 1))
                    if l < len(LEVELS):
                        o, k = (halves(v, LEVELS[l], d, "k") for v in (lev_k[:, l, :], key[:, d, :]))
                    elif l == len(LEVELS):
                        o, k = base_k[:, :], key[:, d, :]
                    else:
                        o, k = st_k[:, ST[d]["k"]], key[:, d, ST[d]["k"]]
                    nc.gpsimd.tensor_tensor(o, o, k, ALU.mult).then_inc(k_side, 1)

            def head(h):
                for d in range(2):
                    key_scale(h, d)
                    key_sides(h, d)
                pool.wait_ge(bias_in, 16 * h + 16)
                if not isinstance(h, int):
                    pool.wait_ge(s_biased, 4 * h)
                for kind in range(3):
                    d = (KIND.index(kind) * QC - KEY_COL[KIND.index(kind)])
                    v = bias[:, :, KW - d:KW - d + KC].rearrange("p a j -> p j a")
                    w = m_win[:, kind, :].rearrange("p (j a) -> p j a", a=1).to_broadcast([P, KC, KH])
                    nc.gpsimd.tensor_tensor(bias_w[:, kind], v, w, ALU.add).then_inc(bias_ready, 1)

            head(0)
            with pool.Fori(1, H) as h:
                head(h)

            pool.wait_ge(za_stored, 16 * (H - 1))
            pool.wait_ge(za_part, H)
            for q in range(H):
                if q == 2:
                    pool.wait_ge(normed, 3 * H)
                    pool.dma_start(z_dram[H - 1], z_a[:, :]).then_inc(za_last, 16)
                if q == 3:
                    pool.wait_ge(za_last, 16)
                if q == 4:
                    pool.wait_ge(zb_stored, 16 * (H - 1))
                if q == 6:
                    pool.wait_ge(zb_ready, H)
                    pool.dma_start(z_dram[2 * H - 1], z_b[:, :]).then_inc(zb_last, 16)
                if q == 7:
                    pool.wait_ge(zb_last, 16)
                if q >= 2:
                    pool.wait_ge(z_lo_done, 2 * (q - 1))
                pool.dma_start(back[:, q % 2], z_dram[2 * q:2 * q + 2].rearrange("f p s -> p f s")).then_inc(z_in[q % 2], 16)

            def bring(n, src):
                if n >= 2:
                    pool.wait_ge(a_lo_done, 2 * (n - 1))
                q = n % (KT // 2)
                pool.dma_start(back[:, n % 2], src[2 * q:2 * q + 2].rearrange("f p s -> p f s")).then_inc(a_in[n % 2], 16)

            for n in range(KT // 2):
                pool.wait_ge(y_stored, 16 * (KT - 3 if n < KT // 2 - 2 else KT - 2 if n < KT // 2 - 1 else KT))
                bring(n, y_dram)
            pool.wait_ge(y_ready, KT)
            pool.dma_start(p_in[:, :, :], p_v).then_inc(p_landed, 16)
            pool.wait_ge(x2t_stored, 16 * 3)
            for n in range(KT // 2, KT):
                if n == KT // 2 + 2:
                    pool.wait_ge(x2_ready, 16)
                    pool.dma_start(x2_dram[3], x2g[:, :, :].rearrange("p t j -> p (t j)")).then_inc(x2_last, 16)
                if n == KT - 2:
                    pool.wait_ge(x2t_ready, 16)
                    pool.dma_start(x2t_dram[12:16].rearrange("f p s -> p f s"), x2t[:, :, :]).then_inc(x2t_last, 16)
                    pool.wait_ge(x2t_last, 16)
                bring(n, x2t_dram)
            pool.wait_ge(x2_last, 16)

        @block.scalar
        def _(act):
            A = nc.scalar.activation

            act.wait_ge(pool_ready, 1)
            A(mean_w[:, :], mean_in[:, :], ACT.Copy).then_inc(mean_ready, 1)
            act.wait_ge(eps_ready, 1)
            for t in range(NT):
                if t == NT - 1:
                    split_hi(act, Units(0), 0)
                act.wait_ge(x_ready[t], 16)
                if t:
                    act.wait_ge(x_sumsq, t)
                A(x_sq[:, :], x_in[:, t, :], ACT.Square, accum_out=stat[:, 0, t:t + 1]).then_inc(x_sumsq, 1)
                act.wait_ge(x_sumsq, t + 1)
                A(stat[:, 1, t:t + 1], stat[:, 0, t:t + 1], ACT.Sqrt, bias=eps_c[:, :], scale=1.0 / D).then_inc(x_root, 1)
            act.wait_ge(const_in, 64)
            for k in range(KT):
                if k == 6:
                    split_hi(act, Units(0), 1)
                act.wait_ge(h_turned, k + 1)
                A(act_hi[:, k, :], ax_ps[:, k % 5, :], ACT.Copy, scale=norm_c[:, k:k + 1]).then_inc(h_hi, 1)

            def chain(h, d):
                act.wait_ge(forget, 4 * h + (2 * d + 2))
                A(logf[:, :], logf[:, :], ACT.Ln).then_inc(log_ready, 1)
                if not (isinstance(h, int) and d == 0):
                    act.wait_ge(intra_done, 2 * h + d)
                if not isinstance(h, int) and d == 0:
                    act.wait_ge(lev_done, h)
                    act.wait_ge(o_done, h)
                decays(h, d, 0, 2)

            def decays(h, d, first, end):
                for n in range(first, end):
                    l = ORDER[n]
                    act.wait_ge(dif_ready, 12 * h + (6 * d + n + 1))
                    e = dif[:, n % 2, :]
                    if l < len(LEVELS):
                        for side, sign, o in (("q", 1.0, lev_q), ("k", -1.0, lev_k)):
                            last = A(halves(o[:, l, :], LEVELS[l], d, side), halves(e, LEVELS[l], d, side),
                                     ACT.Exp, scale=sign)
                    elif l == len(LEVELS):
                        A(base_q[:, :], e, ACT.Exp)
                        last = A(base_k[:, :], e, ACT.Exp, scale=-1.0)
                    else:
                        v = cum[:, :].rearrange("p (c u) -> p c u", u=CHUNK)
                        r = (CHUNK - 1) * (1 - d)
                        A(tot[:, d, :], v[:, :, r], ACT.Exp)
                        A(st_q[:, d, ST[d]["q"]], cum[:, ST[d]["q"]], ACT.Exp)
                        last = A(st_k[:, ST[d]["k"]], dif[:, n % 2, ST[d]["k"]], ACT.Exp, scale=-1.0)
                    last.then_inc(dec_ready, 1)

            def keys_t(h, d):
                act.wait_ge(intra_done, 2 * h + (d + 1))
                if not (isinstance(h, int) and d == 0):
                    act.wait_ge(upd_done, 2 * h + d)
                A(st_kt[:, :], ax_ps[:, 3, 0:3 * P], ACT.Copy).then_inc(kt_ready, 1)

            def root(h, m):
                act.wait_ge(ms_done, 3 * h + (m + 1))
                if not (isinstance(h, int) and h == 0 and m == 0):
                    act.wait_ge(normed, 3 * h + m)
                A(rms[:, :], ax_ps[:, MS_BANK[m], :], ACT.Sqrt, bias=eps_c[:, :]).then_inc(root_ready, 1)

            def squares_hi(h, m):
                A(squares[:, 0, :], temp[:, :], ACT.Copy).then_inc(sq_hi_done, 1)

            def tile(h, j):
                ps = mm_ps[:, j % 3, :]
                act.wait_ge(unit_done, NU * h + (2 * j + 2))
                if j in (HF, HB):
                    A(logf[:, :], ps, ACT.Sigmoid)
                    last = A(key[:, j - HF, :], ps, ACT.Sigmoid, scale=-1.0)
                elif j in (HI, NV):
                    if j == NV or not isinstance(h, int):
                        act.wait_ge(vt_done, 2 * h + (1 if j == NV else 0))
                    if j == NV:
                        last = A(columns_of(v_t[:, :]), by_column(ps), ACT.Copy)
                    else:
                        last = A(v_t[:, :], ps, ACT.Copy)
                elif j in (NQ, NK):
                    if j == NK:
                        act.wait_ge(ms_done, 3 * h + 1)
                    else:
                        act.wait_ge(tile_dve, 5 * h + 2)
                    last = A(temp[:, :], ps, ACT.Square)
                else:
                    if j == HG:
                        act.wait_ge(tile_dve, 5 * h + 1)
                    elif j == HQ and not isinstance(h, int):
                        act.wait_ge(tile_dve, 5 * h)
                    last = A(temp[:, :], ps, ACT.Sigmoid)
                last.then_inc(tile_act, 1)
                if j in (NQ, NK):
                    act.wait_ge(tile_act, 9 * h + (j + 1))
                    squares_hi(h, j - NQ)

            def late(i, g):
                if i == 0:
                    root(g, 2)
                    tile(g, NG)
                    act.wait_ge(vt_done, 2 * g + 2)
                    A(n_v[:, :, :].rearrange("p n d -> p (n d)"),
                      ax_ps[:, 2:4, :].rearrange("p a s -> p (a s)")[:, 0:len(V_COL) * P], ACT.Copy).then_inc(val_ready, 1)
                if 1 <= i <= 4:
                    t = i - 1
                    act.wait_ge(s_neg, 4 * g + (t + 1))
                    A(prob[:, t % 2, :], prob[:, t % 2, :], ACT.Exp, bias=soft[:, 1, t:t + 1],
                      accum_out=soft[:, 2, t:t + 1]).then_inc(e_done, 1)
                if 3 <= i <= 6:
                    t = i - 3
                    act.wait_ge(pt_done, 4 * g + (t + 1))
                    if t >= 2:
                        act.wait_ge(pv_done, 4 * g + (t - 1))
                    A(prob_t[:, t % 2, :], ax_ps[:, 2 + t % 2, 0:KH * KC], ACT.Copy).then_inc(pt_ready, 1)

            def head(h):
                us = Units(0, NU, h)
                for i in range(NU):
                    split_hi(act, us, i + AHEAD)
                    if not isinstance(h, int):
                        late(i, h - 1)
                    elif i == 0:
                        act.wait_ge(lb_step, 1)
                        A(lb_col[:, 2, :], lb_col[:, 1, :], ACT.Exp).then_inc(lb_step, 1)
                    if i == 9:
                        keys_t(h, 0)
                    if i == 12:
                        keys_t(h, 1)
                    if i == 10:
                        act.wait_ge(vt_done, 2 * h + 1)
                        A(val[:, :], ax_ps[:, 3, :], ACT.Copy).then_inc(val_ready, 1)
                    if i in (14, 16):
                        root(h, (i - 14) // 2)
                    if i == 16:
                        act.wait_ge(o_done, h + 1)
                        act.wait_ge(ms_done, 3 * h + 2)
                        A(temp[:, :], ax_ps[:, 4, :], ACT.Square).then_inc(osq_ready, 1)
                        act.wait_ge(osq_ready, h + 1)
                        squares_hi(h, 2)
                    if i % 2 == 0 and i >= 2:
                        tile(h, i // 2 - 1)
                    if i in (5, 9):
                        chain(h, i // 9)
                    if i in (6, 7, 10, 11):
                        n = 2 if i % 4 == 2 else 4
                        decays(h, i // 10, n, n + 2)

            head(0)
            with act.Fori(1, H) as h:
                head(h)

            def merge_gate(n, b, slot, done):
                act.wait_ge(unit_done, done)
                if not (isinstance(n, int) and n < 2):
                    act.wait_ge(y_ready, n - 1)
                A(g_ab[:, slot, b, :], mm_ps[:, b, :], ACT.Sigmoid).then_inc(gate_ready, 1)

            def z_hi_tiles(k0, k1):
                for k in range(k0, k1):
                    act.wait_ge(z_in[k // 2 % 2], 16 * (k // 4 + 1))
                    A(z_hi[k // H][:, k % H, :], back[:, k // 2 % 2, k % 2, :], ACT.Copy).then_inc(z_hi_done, 1)

            us = Units(U_MERGE)
            for i in range(8):
                split_hi(act, us, i + AHEAD)
                late(i, H - 1)
                if i:
                    z_hi_tiles(i if i > 1 else 0, i + 1)
                if i in (2, 4):
                    merge_gate(0, i // 2 - 1, 0, us.num(i))
                if i == 6:
                    merge_gate(1, 0, 1, us.num(i))

            def merge_pair(r, is_first=False):
                us = Units(U_MERGE + 8, 12, r)
                for i in range(12):
                    if is_first and i == 0:
                        act.wait_ge(zb_ready, H)
                        z_hi_tiles(H, H + 4)
                    split_hi(act, us, i + AHEAD)
                    if is_first and i == 0:
                        z_hi_tiles(H + 4, 2 * H)
                    if i in (0, 4, 6, 10):
                        n, b, s = {0: (1, 1, 1), 4: (2, 0, 0), 6: (2, 1, 0), 10: (3, 0, 1)}[i]
                        merge_gate(r * 2 + n, b, s, us.num(i))

            merge_pair(0, is_first=True)
            with act.Fori(1, KT // 2 - 1) as r:
                merge_pair(r)

            def act_hi_tiles(k0, k1, phase):
                for k in range(k0, k1):
                    n = phase * (KT // 2) + k // 2
                    act.wait_ge(a_in[n % 2], 16 * (n // 2 + 1))
                    A(act_hi[:, k, :], back[:, n % 2, k % 2, :], ACT.Copy).then_inc(a_hi_done, 1)

            us = Units(U_OUT - 4)
            for i in range(4):
                split_hi(act, us, i + AHEAD, 1024 if i < 2 else out_width(i - 2))
                if i == 0:
                    merge_gate(KT - 1, 1, 1, us.num(0))
                    act.wait_ge(unit_done, U_OUT - 4)
                act_hi_tiles(4 * i, min(4 * i + 4, 14), 0)

            def token_squares(c):
                for t in range(NT):
                    act.wait_ge(x2_ready, 4 * c + (t + 1))
                    if not (isinstance(c, int) and c == 0 and t == 0):
                        act.wait_ge(x2_sq, 4 * c + t)
                    if t == 0 and not (isinstance(c, int) and c == 0):
                        act.wait_ge(ss_sum, c + 1)
                    A(junk[:, :], x2g[:, t, :], ACT.Square, accum_out=ssq[:, t:t + 1]).then_inc(x2_sq, 1)

            def turn_out(c):
                act.wait_ge(pn_in, 16 * c + 16)
                for f in range(4):
                    act.wait_ge(x2_turned, 4 * c + (f + 1))
                    A(x2t[:, f, :], ax_ps[:, 1 + f, :], ACT.Copy, scale=pn_c[:, f:f + 1]).then_inc(x2t_ready, 1)

            def out_group(c, is_first=False):
                us = Units(U_OUT, 6, c)
                for i in range(6):
                    if i == 4 and isinstance(c, int) and c == 3:
                        act.wait_ge(pw_raw, 16)
                    split_hi(act, us, i + AHEAD, out_width(i + AHEAD))
                    if is_first and i == 1:
                        act_hi_tiles(14, KT, 0)
                    if is_first and i == 3:
                        for k in range(PT):
                            act.wait_ge(p_turned, k + 1)
                            A(p_hi[:, k, :], ax_ps[:, 1 + k, :], ACT.Copy).then_inc(p_hi_done, 1)
                    if not is_first and i == 1:
                        turn_out(c - 1)
                if not is_first:
                    act.wait_ge(x2t_stored, 16 * c)
                token_squares(c)

            out_group(0, is_first=True)
            with act.Fori(1, 3) as c:
                out_group(c)
            out_group(3)
            act.wait_ge(unit_done, U_PLE)
            act_hi_tiles(0, 4, 1)

            def ple_group(c, is_first=False, is_last=False):
                us = Units(U_PLE, 6, c)
                for i in range(6):
                    if not (is_last and i + AHEAD >= 6):
                        if i == 4:
                            act.wait_ge(pw_raw, 16 * c + 32)
                        split_hi(act, us, i + AHEAD, 1536)
                    if is_first and i == 1:
                        act.wait_ge(ss_sum, 5)
                        A(stat[:, 1, :], stat[:, 3, :], ACT.Sqrt, bias=eps_c[:, :], scale=1.0 / D).then_inc(rstd_root, 1)
                    if is_first and i == 2:
                        turn_out(3)
                    if is_first and i < 4:
                        act_hi_tiles(4 + 3 * i, 7 + 3 * i, 1)
                act.wait_ge(rstd_ready, 1)
                for t in range(NT):
                    acc_full(act, us, c + 4, t)
                    if not (isinstance(c, int) and c == 0):
                        act.wait_ge(res_ready, 4 * c - 3 + t)
                    A(g_sig[:, t, :], acc(t), ACT.Sigmoid, scale=stat[:, 2, t:t + 1]).then_inc(g_ready, 1)

            ple_group(0, is_first=True)
            with act.Fori(1, 3) as c:
                ple_group(c)
            ple_group(3, is_last=True)

        @block.vector
        def _(dve):
            TT, STT, TS = nc.vector.tensor_tensor, nc.vector.scalar_tensor_tensor, nc.vector.tensor_scalar
            nc.vector.memset(eps_c[:, :], EPS).then_inc(eps_ready, 1)
            for t in range(NT):
                if t == NT - 1:
                    split_lo(dve, Units(0), 0)
                dve.wait_ge(x_root, t + 1)
                nc.vector.reciprocal(stat[:, 2, t:t + 1], stat[:, 1, t:t + 1]).then_inc(x_recip, 1)
                dve.wait_ge(x_recip, t + 1)
                n = 4 * P if t == NT - 1 else D
                TS(x_in[:, t, 0:n], x_in[:, t, 0:n], stat[:, 2, t:t + 1], None, ALU.mult).then_inc(x_normed, 1)
            TS(x_in[:, NT - 1, n:D], x_in[:, NT - 1, n:D], stat[:, 2, NT - 1:NT], None, ALU.mult).then_inc(x_tail, 1)
            dve.wait_ge(const_in, 64)
            for k in range(KT):
                if k == 6:
                    split_lo(dve, Units(0), 1)
                dve.wait_ge(h_hi, k + 1)
                STT(act_lo[:, k, :], ax_ps[:, k % 5, :], norm_c[:, k:k + 1], act_hi[:, k, :].bitcast(F32),
                    ALU.mult, ALU.subtract).then_inc(h_lo, 1)
            def lower_bounds():
                dve.wait_ge(lb_in, 32)
                TT(lb_col[:, 1, :], lb_col[:, 0, :], lb_col[:, 0, :], ALU.subtract).then_inc(lb_step, 1)
                dve.wait_ge(lb_step, 2)
                nc.vector.reciprocal(lb_col[:, 3, :], lb_col[:, 2, :]).then_inc(lb_step, 1)
                dve.wait_ge(lb_step, 3)
                TT(lb_col[:, 0, :], lb_col[:, 2, :], lb_col[:, 3, :], ALU.mult).then_inc(lb_step, 1)
                dve.wait_ge(lb_step, 4)
                v = lb_col[:, 0, :].rearrange("p (d h) -> p h d", d=2)
                TT(low[:, :, 0:2], v, v, ALU.subtract).then_inc(lb_step, 1)
                dve.wait_ge(lb_step, 5)
                TS(low[:, :, 2:4], low[:, :, 0:2], -1.0, 1.0, ALU.mult, ALU.add).then_inc(lb_step, 1)

            def forget_gate(h, d):
                dve.wait_ge(tile_act, 9 * h + (HF + d + 1))
                dve.wait_ge(low_ready, h + 1)
                TS(logf[:, :], logf[:, :], low_h[:, 2 + d:3 + d], low_h[:, d:d + 1],
                   ALU.mult, ALU.add).then_inc(forget, 1)
                dve.wait_ge(forget, 4 * h + (2 * d + 1))
                TS(logf[:, :], logf[:, :], F_MIN, None, ALU.max).then_inc(forget, 1)

            def chain(h, d, first=0):
                if first == 0:
                    dve.wait_ge(log_ready, 2 * h + (d + 1))
                    f, c = logf[:, :], cum[:, :]
                    if d:
                        f, c = f[:, ::-1], c[:, ::-1]
                    nc.vector.tensor_tensor_scan(c, reset[:, :], f, 0.0, ALU.mult, ALU.add).then_inc(cum_ready, 1)
                    dve.wait_ge(cum_ready, 2 * h + (d + 1))

                def distance(n):
                    l = ORDER[n]
                    if not (isinstance(h, int) and d == 0 and n < 2):
                        dve.wait_ge(dec_ready, 12 * h + (6 * d + n - 1))
                    v, ref, w = reference(cum[:, :], l, d)
                    TT(dif[:, n % 2, :].rearrange("p (b w) -> p b w", w=w), v, ref, ALU.subtract).then_inc(dif_ready, 1)

                def query_side(n):
                    l = ORDER[n]
                    dve.wait_ge(dec_ready, 12 * h + (6 * d + n + 1))
                    if l < len(LEVELS):
                        o, q = (halves(v, LEVELS[l], d, "q") for v in (lev_q[:, l, :], qry[:, :]))
                    elif l == len(LEVELS):
                        o, q = base_q[:, :], qry[:, :]
                    else:
                        o, q = st_q[:, d, ST[d]["q"]], qry[:, ST[d]["q"]]
                    TT(o, o, q, ALU.mult).then_inc(q_side, 1)

                if first == 0:
                    distance(0)
                    distance(1)
                for n in range(first, first + 2):
                    query_side(n)
                    if n + 2 < NL:
                        distance(n + 2)

            def place(h, d, bank, mask, written, done):
                dve.wait_ge(pool_step, POOL_STEPS)
                written()
                o, s = (v.rearrange("p (t u) -> p t u", t=NT) for v in (att[:, d, :], ax_ps[:, bank, :]))
                k = mask.bitcast(U32).rearrange("p (a u) -> p a u", a=1).to_broadcast([P, NT, CHUNK])
                nc.vector.copy_predicated(o, k, s).then_inc(done, 1)

            def base_products(h, d):
                def written():
                    dve.wait_ge(intra_done, 2 * h + (d + 1))
                    if d:
                        dve.wait_ge(att_part[1], h + 1)
                    elif not isinstance(h, int):
                        dve.wait_ge(att_ready, h)
                place(h, 1 - d, 2, m_base[:, d, :], written, base_part)

            def level_products(h, l):
                def written():
                    if l == 0:
                        dve.wait_ge(intra_done, 2 * h + 2)
                        if not isinstance(h, int):
                            dve.wait_ge(att_ready, h)
                    elif l == 2:
                        dve.wait_ge(lev_done, h + 1)
                        dve.wait_ge(base_part, 2 * h + 2)
                    else:
                        dve.wait_ge(att_part[l - 1], h + 1)
                place(h, 0, l % 2, m_lev[:, l, :], written, att_part[l])

            def att_total(h):
                dve.wait_ge(att_part[3], h + 1)
                dve.wait_ge(base_part, 2 * h + 1)
                TT(att_sum[:, :], att[:, 0, :], att[:, 1, :], ALU.add).then_inc(att_ready, 1)

            def states(h, d):
                dve.wait_ge(upd_done, 2 * h + (d + 1))
                if not isinstance(h, int):
                    dve.wait_ge(o_done, h)
                for n in range(3):
                    u = ax_ps[:, 4, n * P:(n + 1) * P]
                    if n == 0:
                        nc.vector.tensor_copy(state[:, d, 0, :], u).then_inc(state_ready, 1)
                    else:
                        dve.wait_ge(state_ready, 6 * h + (3 * d + n))
                        ch = FEED[d][n]
                        STT(state[:, d, n, :], state[:, d, n - 1, :], tot[:, d, ch:ch + 1], u,
                            ALU.mult, ALU.add).then_inc(state_ready, 1)

            def squares_lo(h, m):
                dve.wait_ge(sq_hi_done, 3 * h + (m + 1))
                TT(squares[:, 1, :], temp[:, :], squares[:, 0, :].bitcast(F32), ALU.subtract).then_inc(sq_lo_done, 1)

            def normalise(h, m):
                dve.wait_ge(root_ready, 3 * h + (m + 1))
                nc.vector.reciprocal(rms[:, :], rms[:, :]).then_inc(rinv_ready, 1)
                dve.wait_ge(rinv_ready, 3 * h + (m + 1))
                v = (n_q, n_k, z_a)[m][:, :]
                r = rms[:, :]
                if m < 2:
                    v, r = (queries_of, columns_of)[m](v), by_column(r)
                TT(v, v, r, ALU.mult).then_inc(normed, 1)

            def tile(h, j):
                ps = mm_ps[:, j % 3, :]
                dve.wait_ge(unit_done, NU * h + (2 * j + 2))
                dve.wait_ge(tile_act, 9 * h + (j + 1))
                if j in (NQ, NK):
                    if not isinstance(h, int):
                        dve.wait_ge(s_done, 4 * h)
                    o = queries_of(n_q[:, :]) if j == NQ else columns_of(n_k[:, :])
                    TS(o, by_column(ps), cols[:, 1 + j - NQ:2 + j - NQ], None,
                       ALU.mult).then_inc(tile_dve, 1)
                else:
                    o = {HQ: qry, HG: gate, NG: n_gate}[j]
                    TT(o[:, :], ps, temp[:, :], ALU.mult).then_inc(tile_dve, 1)

            def late(i, g):
                if i == 0:
                    normalise(g, 2)
                    tile(g, NG)
                if 1 <= i <= 4:
                    t = i - 1
                    dve.wait_ge(s_done, 4 * g + (t + 1))
                    if t == 0:
                        dve.wait_ge(bias_ready, 3 * g + 3)
                    if t >= 2:
                        dve.wait_ge(pt_done, 4 * g + (t - 1))
                    STT(prob[:, t % 2, :], ax_ps[:, t % 2, 0:KH * KC], SCALE, bias_w[:, KIND[t]].rearrange("p j a -> p (j a)"),
                        ALU.mult, ALU.add).then_inc(s_biased, 1)
                    dve.wait_ge(s_biased, 4 * g + (t + 1))
                    nc.vector.tensor_reduce(soft[:, 0, t:t + 1], prob[:, t % 2, :], AX.X, ALU.max).then_inc(s_max, 1)
                    dve.wait_ge(s_max, 4 * g + (t + 1))
                    TS(soft[:, 1, t:t + 1], soft[:, 0, t:t + 1], -1.0, None, ALU.mult).then_inc(s_neg, 1)
                if 2 <= i <= 5:
                    t = i - 2
                    dve.wait_ge(e_done, 4 * g + (t + 1))
                    nc.vector.reciprocal(soft[:, 3, t:t + 1], soft[:, 2, t:t + 1]).then_inc(e_recip, 1)
                    dve.wait_ge(e_recip, 4 * g + (t + 1))
                    TS(prob[:, t % 2, :], prob[:, t % 2, :], soft[:, 3, t:t + 1], None, ALU.mult).then_inc(p_ready, 1)
                if i == 7:
                    dve.wait_ge(pv_done, 4 * g + 4)
                    TT(by_column(z_b[:, :]), queries_of(ax_ps[:, 4, :]), by_column(n_gate[:, :]), ALU.mult).then_inc(zb_ready, 1)

            def head(h):
                us = Units(0, NU, h)
                for i in range(NU):
                    split_lo(dve, us, i + AHEAD)
                    if not isinstance(h, int):
                        late(i, h - 1)
                    elif i == 0:
                        lower_bounds()
                    if i == 2 and isinstance(h, int):
                        dve.wait_ge(pool_step, POOL_STEPS)
                        nc.vector.memset(att[:, :, :], 0.0).then_inc(att_zero, 1)
                        dve.wait_ge(att_zero, 1)
                    if i == 12:
                        level_products(h, 0)
                        level_products(h, 1)
                    if i in (12, 14, 16):
                        squares_lo(h, (i - 12) // 2)
                    if i in (2, 10, 12, 14):
                        tile(h, i // 2 - 1)
                    if i == 3:
                        if isinstance(h, int):
                            dve.wait_ge(lb_step, 6)
                        else:
                            dve.wait_ge(key_ready, 2 * h)
                        TS(low_h[:, :], low[:, bass.ds(h, 1), :].rearrange("p a c -> p (a c)"), 1.0, None,
                           ALU.mult).then_inc(low_ready, 1)
                    if i in (4, 6):
                        forget_gate(h, i // 2 - 2)
                    if i == 9:
                        base_products(h, 0)
                    if i == 12:
                        base_products(h, 1)
                    if i == 13:
                        level_products(h, 2)
                        level_products(h, 3)
                        att_total(h)
                    if i in (5, 9):
                        chain(h, i // 9)
                    if i in (6, 7, 10, 11):
                        chain(h, i // 10, first=2 if i % 4 == 2 else 4)
                    if i == 17 and not isinstance(h, int):
                        dve.wait_ge(zb_stored, 16 * h)
                    if i == 11:
                        states(h, 0)
                    if i == 14:
                        states(h, 1)
                        normalise(h, 0)
                    if i == 16:
                        dve.wait_ge(osq_ready, h + 1)
                        if not isinstance(h, int):
                            dve.wait_ge(za_stored, 16 * h)
                        STT(z_a[:, :], ax_ps[:, 4, :], cols[:, 0:1], gate[:, :], ALU.mult, ALU.mult).then_inc(za_part, 1)
                        normalise(h, 1)

            head(0)
            with dve.Fori(1, H) as h:
                head(h)

            def merge_y(n, slot, us, i):
                dve.wait_ge(gate_ready, 2 * n + 2)
                for b in range(2):
                    dve.wait_ge(unit_done, us.num(i + b) + 1)
                    TT(g_ab[:, slot, b, :], branch_ps(slot, b), g_ab[:, slot, b, :], ALU.mult).then_inc(y_part, 1)
                dve.wait_ge(y_part, 2 * n + 2)
                if not (isinstance(n, int) and n == 0):
                    dve.wait_ge(y_stored, 16 * n)
                TT(y_out[:, :], g_ab[:, slot, 0, :], g_ab[:, slot, 1, :], ALU.add).then_inc(y_ready, 1)

            def z_lo_tiles(k0, k1):
                for k in range(k0, k1):
                    dve.wait_ge(z_hi_done, k + 1)
                    TT(z_lo[k // H][:, k % H, :], back[:, k // 2 % 2, k % 2, :], z_hi[k // H][:, k % H, :].bitcast(F32),
                       ALU.subtract).then_inc(z_lo_done, 1)

            us = Units(U_MERGE)
            for i in range(8):
                split_lo(dve, us, i + AHEAD)
                late(i, H - 1)
                if i:
                    z_lo_tiles(i if i > 1 else 0, i + 1)

            def merge_pair(r, is_first=False):
                us = Units(U_MERGE + 8, 12, r)
                for i in range(12):
                    if is_first and i == 0:
                        z_lo_tiles(H, H + 4)
                    split_lo(dve, us, i + AHEAD)
                    if is_first and i == 0:
                        z_lo_tiles(H + 4, 2 * H)
                    if i in (2, 8):
                        merge_y(r * 2 + i // 8, i // 8, us, i - 2)

            merge_pair(0, is_first=True)
            with dve.Fori(1, KT // 2 - 1) as r:
                merge_pair(r)

            def act_lo_tiles(k0, k1, phase):
                for k in range(k0, k1):
                    n = phase * (KT // 2) + k // 2
                    dve.wait_ge(a_hi_done, phase * KT + k + 1)
                    TT(act_lo[:, k, :], back[:, n % 2, k % 2, :], act_hi[:, k, :].bitcast(F32),
                       ALU.subtract).then_inc(a_lo_done, 1)

            us = Units(U_OUT - 4)
            for i in range(4):
                split_lo(dve, us, i + AHEAD, 1024 if i < 2 else out_width(i - 2))
                if i == 2:
                    merge_y(KT - 2, 0, us, 0)
                act_lo_tiles(4 * i, min(4 * i + 4, 14), 0)
            merge_y(KT - 1, 1, us, 2)

            def running_sum(c):
                dve.wait_ge(x2_sq, 4 * c)
                dve.wait_ge(ss_sum, c)
                TT(stat[:, 3, :], stat[:, 3, :], ssq[:, :], ALU.add).then_inc(ss_sum, 1)

            def residual(c, us):
                dve.wait_ge(xg_in, 16 * c + 16)
                if not (isinstance(c, int) and c == 0):
                    dve.wait_ge(x2_stored, 16 * c)
                    dve.wait_ge(x2_turned, 4 * c)
                for t in range(NT):
                    acc_full(dve, us, c, t)
                    TT(x2g[:, t, :], acc(t), xg[:, t, :], ALU.add).then_inc(x2_ready, 1)

            def out_group(c, is_first=False):
                us = Units(U_OUT, 6, c)
                for i in range(6):
                    split_lo(dve, us, i + AHEAD, out_width(i + AHEAD))
                    if is_first and i == 1:
                        act_lo_tiles(14, KT, 0)
                    if is_first and i == 3:
                        for k in range(PT):
                            dve.wait_ge(p_hi_done, k + 1)
                            TT(p_lo[:, k, :], ax_ps[:, 1 + k, :], p_hi[:, k, :].bitcast(F32),
                               ALU.subtract).then_inc(p_lo_done, 1)
                    if not is_first and i == 1:
                        running_sum(c)
                residual(c, us)

            nc.vector.memset(stat[:, 3, :], 0.0).then_inc(ss_sum, 1)
            out_group(0, is_first=True)
            with dve.Fori(1, 4) as c:
                out_group(c)
            act_lo_tiles(0, 4, 1)
            running_sum(4)

            def ple_group(c, is_first=False, is_last=False):
                us = Units(U_PLE, 6, c)
                for i in range(6):
                    if not (is_last and i + AHEAD >= 6):
                        split_lo(dve, us, i + AHEAD, 1536)
                    if i == 1:
                        if not (isinstance(c, int) and c == 0):
                            dve.wait_ge(res_ready, 4 * c)
                        for t in range(NT):
                            dve.wait_ge(unit_done, us.num(1))
                            nc.vector.tensor_copy(p_w[:, t, :], ax_ps[:, 1 + t, :]).then_inc(pw_ready, 1)
                    if is_first and i == 2:
                        dve.wait_ge(rstd_root, 1)
                        nc.vector.reciprocal(stat[:, 2, :], stat[:, 1, :]).then_inc(rstd_ready, 1)
                    if is_first and i < 4:
                        act_lo_tiles(4 + 3 * i, 7 + 3 * i, 1)
                dve.wait_ge(x2_in, 16 * c + 16)
                dve.wait_ge(pw_ready, 4 * c + 4)
                if not (isinstance(c, int) and c == 0):
                    dve.wait_ge(out_stored, 64 * c)
                for t in range(NT):
                    dve.wait_ge(g_ready, 4 * c + (t + 1))
                    TT(p_w[:, t, :], p_w[:, t, :], g_sig[:, t, :], ALU.mult).then_inc(gp_ready, 1)
                    dve.wait_ge(gp_ready, 4 * c + (t + 1))
                    TT(res[:, t, :], p_w[:, t, :], xg[:, t, :], ALU.add).then_inc(res_ready, 1)

            ple_group(0, is_first=True)
            with dve.Fori(1, 3) as c:
                ple_group(c)
            ple_group(3, is_last=True)

        @block.tensor
        def _(pe):
            MM = nc.tensor.matmul

            def turn_h(k):
                if k >= 5:
                    pe.wait_ge(h_lo, k - 4)
                for t in range(NT):
                    mm = nc.tensor.transpose(ax_ps[:, k % 5, t * P:(t + 1) * P], x_in[:, t, k * P:(k + 1) * P], ident[:, :])
                mm.then_inc(h_turned, 1)

            def columns(us, i, bank, k0, kn, start, stop, m_hi, m_lo, first=False, split=None):
                pe.wait_ge(lo_done, us.num(i) + 1)
                s = us.slot(i)
                for k in range(kn):
                    if first:
                        if k0 + k + 4 < KT:
                            turn_h(k0 + k + 4)
                        pe.wait_ge(h_lo, k0 + k + 1)
                    if split is not None:
                        pe.wait_ge(z_lo_done, split + k + 1)
                    wh, wl = w_hi[:, s, k * P:(k + 1) * P], w_lo[:, s, k * P:(k + 1) * P]
                    MM(bank, wh, m_hi[:, k0 + k, :], start=start and k == 0, stop=False)
                    MM(bank, wh, m_lo[:, k0 + k, :], start=False, stop=False)
                    mm = MM(bank, wl, m_hi[:, k0 + k, :], start=False, stop=stop and k == kn - 1)
                mm.then_inc(unit_done, 1)

            def tile_free(h, j):
                if isinstance(h, int) and h == 0 and j < 3:
                    return
                pj = (j - 3) % 9
                pe.wait_ge(tile_act, 9 * h + (j - 2))
                if pj in DREAD:
                    pe.wait_ge(tile_dve, 5 * h + (DREAD[pj] - (5 if j < 3 else 0)))

            def intra(h, d):
                for side in (q_side, k_side):
                    pe.wait_ge(side, 12 * h + (10 if d else 2))
                if d:
                    pe.wait_ge(base_part, 2 * h + 1)
                    pe.wait_ge(val_ready, 2 * h + 1)
                elif not isinstance(h, int):
                    pe.wait_ge(pt_ready, 4 * h)
                if d:
                    levels(0)
                for t in range(NT):
                    c = slice(t * P, (t + 1) * P)
                    MM(ax_ps[:, 2, c], base_k[:, c], base_q[:, c], start=True, stop=True)
                for n, ch in enumerate(FEED[d]):
                    mm = nc.tensor.transpose(ax_ps[:, 3, n * P:(n + 1) * P], st_k[:, ch * P:(ch + 1) * P], ident[:, :])
                mm.then_inc(intra_done, 1)

            def levels(first):
                for l in (first, first + 1):
                    for t in range(NT):
                        c = slice(t * P, (t + 1) * P)
                        mm = MM(ax_ps[:, l % 2, c], lev_k[:, l, c], lev_q[:, l, c], start=True, stop=True)
                return mm

            def updates(h, d):
                pe.wait_ge(kt_ready, 2 * h + (d + 1))
                if d:
                    pe.wait_ge(state_ready, 6 * h + 3)
                else:
                    pe.wait_ge(val_ready, 2 * h + 1)
                    if not isinstance(h, int):
                        pe.wait_ge(zb_ready, h)
                for n, ch in enumerate(FEED[d]):
                    mm = MM(ax_ps[:, 4, n * P:(n + 1) * P], st_kt[:, n * P:(n + 1) * P], val[:, ch * P:(ch + 1) * P],
                            start=True, stop=True)
                mm.then_inc(upd_done, 1)

            def outputs(h):
                pe.wait_ge(att_ready, h + 1)
                pe.wait_ge(state_ready, 6 * h + 6)
                for t in range(NT):
                    c = slice(t * P, (t + 1) * P)
                    terms = [(val[:, c], att_sum[:, c])]
                    if t > 0:
                        terms.append((state[:, 0, t - 1, :], st_q[:, 0, c]))
                    if t < NT - 1:
                        terms.append((state[:, 1, NT - 2 - t, :], st_q[:, 1, c]))
                    for n, (lhs, rhs) in enumerate(terms):
                        mm = MM(ax_ps[:, 4, c], lhs, rhs, start=n == 0, stop=n == len(terms) - 1)
                mm.then_inc(o_done, 1)

            def mean_square(h, m):
                pe.wait_ge(sq_lo_done, 3 * h + (m + 1))
                MM(ax_ps[:, MS_BANK[m], :], mean_w[:, :], squares[:, 0, :], start=True, stop=False)
                MM(ax_ps[:, MS_BANK[m], :], mean_w[:, :], squares[:, 1, :], start=False, stop=True).then_inc(ms_done, 1)

            def turn_v():
                for t in range(NT):
                    c = slice(t * P, (t + 1) * P)
                    mm = nc.tensor.transpose(ax_ps[:, 3, c], v_t[:, c], ident[:, :])
                mm.then_inc(vt_done, 1)

            def turn_windows():
                for n, col in enumerate(V_COL):
                    c = col * ROWS
                    mm = nc.tensor.transpose(ax_ps[:, 2 + n // 4, n % 4 * P:(n % 4 + 1) * P], v_t[:, c:c + P], ident[:, :])
                mm.then_inc(vt_done, 1)

            def late(i, g):
                if i < 4:
                    if i == 0:
                        pe.wait_ge(normed, 3 * g + 2)
                        pe.wait_ge(root_ready, 3 * g + 2)
                    if i == 1:
                        pe.wait_ge(root_ready, 3 * g + 3)
                    if i >= 2:
                        pe.wait_ge(s_biased, 4 * g + (i - 1))
                    MM(ax_ps[:, i % 2, 0:KH * KC], n_q[:, i * P:(i + 1) * P], n_k[:, key_window(i)], start=True, stop=True).then_inc(s_done, 1)
                if 2 <= i <= 5:
                    t = i - 2
                    pe.wait_ge(p_ready, 4 * g + (t + 1))
                    if t == 0:
                        pe.wait_ge(val_ready, 2 * g + 2)
                    if t >= 2:
                        pe.wait_ge(pt_ready, 4 * g + (t - 1))
                    for k in range(2):
                        c = slice(k * P, (k + 1) * P)
                        mm = nc.tensor.transpose(ax_ps[:, 2 + t % 2, c], prob[:, t % 2, c], ident[:, :])
                    mm.then_inc(pt_done, 1)
                if 3 <= i <= 6:
                    t = i - 3
                    pe.wait_ge(pt_ready, 4 * g + (t + 1))
                    if t == 0:
                        pe.wait_ge(za_part, g + 1)
                        pe.wait_ge(osq_ready, g + 1)
                    for k in range(2):
                        mm = MM(ax_ps[:, 4, t * P:(t + 1) * P], n_v[:, V_COL.index(KEY_COL[t] + k * (KC // 2)), :], prob_t[:, t % 2, k * P:(k + 1) * P],
                                start=k == 0, stop=k == 1)
                    mm.then_inc(pv_done, 1)

            def head(h):
                us = Units(0, NU, h)
                for i in range(NU):
                    j = i // 2
                    if i % 2 == 0:
                        tile_free(h, j)
                    columns(us, i, mm_ps[:, j % 3, :], 8 * (i % 2), 8, i % 2 == 0, i % 2 == 1, act_hi, act_lo,
                            first=isinstance(h, int) and i < 2)
                    if not isinstance(h, int):
                        late(i, h - 1)
                    if i == 8:
                        intra(h, 0)
                    if i == 9:
                        pe.wait_ge(tile_act, 9 * h + (HI + 1))
                        pe.wait_ge(kt_ready, 2 * h + 1)
                        turn_v()
                    if i == 10:
                        updates(h, 0)
                    if i == 11:
                        intra(h, 1)
                    if i == 12:
                        pe.wait_ge(q_side, 12 * h + 12)
                        pe.wait_ge(k_side, 12 * h + 12)
                        pe.wait_ge(att_part[1], h + 1)
                        levels(2).then_inc(lev_done, 1)
                    if i == 13:
                        updates(h, 1)
                        pe.wait_ge(mean_ready, 1)
                        pe.wait_ge(base_part, 2 * h + 2)
                        mean_square(h, 0)
                    if i == 15:
                        pe.wait_ge(att_ready, h + 1)
                        mean_square(h, 1)
                        outputs(h)
                    if i == 17:
                        mean_square(h, 2)
                        pe.wait_ge(tile_act, 9 * h + (NV + 1))
                        pe.wait_ge(kt_ready, 2 * h + 2)
                        pe.wait_ge(root_ready, 3 * h + 1)
                        turn_windows()

            pe.wait_ge(pool_step, 2)
            for t in range(NT):
                pe.wait_ge(x_normed, t + 1)
                for k in range(4):
                    mm = nc.tensor.transpose(ax_ps[:, k, t * P:(t + 1) * P], x_in[:, t, k * P:(k + 1) * P], ident[:, :])
                    if t == NT - 1:
                        mm.then_inc(h_turned, 1)
            pe.wait_ge(x_tail, 1)
            head(0)
            with pe.Fori(1, H) as h:
                head(h)

            def gates(us, i, n, after_heads=False):
                for b in range(2):
                    if after_heads:
                        tile_free(H - 1, 9 + b)
                    else:
                        pe.wait_ge(gate_ready, 2 * n + (b - 1))
                    for e in range(2):
                        columns(us, i + 2 * b + e, mm_ps[:, b, :], 8 * e, 8, e == 0, e == 1, act_hi, act_lo)
                        yield

            def run(steps, after=None):
                for k, _ in enumerate(steps):
                    if after:
                        after(k)

            us = Units(U_MERGE)
            run(gates(us, 0, 0, after_heads=True), lambda k: late(k, H - 1))
            run(gates(us, 4, 1), lambda k: late(4 + k, H - 1))

            def branch(us, i, n, slot):
                for b in range(2):
                    if isinstance(n, int) and n < 2:
                        pe.wait_ge(tile_dve, 5 * H)
                        pe.wait_ge(zb_ready, H)
                    elif b == 0:
                        pe.wait_ge(y_part, 2 * n - 2)
                    columns(us, i + b, branch_ps(slot, b), 0, H, True, True, z_hi[b], z_lo[b],
                            split=H * b if isinstance(n, int) and n == 0 else None)

            def merge_pair(r):
                us = Units(U_MERGE + 8, 12, r)
                for e in range(2):
                    branch(us, 6 * e, r * 2 + e, e)
                    run(gates(us, 6 * e + 2, r * 2 + (2 + e)))

            merge_pair(0)
            with pe.Fori(1, KT // 2 - 1) as r:
                merge_pair(r)
            us = Units(U_OUT - 4)
            branch(us, 0, KT - 2, 0)
            branch(us, 2, KT - 1, 1)

            def rows(us, i, terms, last, rounds=1):
                pe.wait_ge(lo_done, us.num(i) + 1)
                s = us.slot(i)
                for t in [n + NT * r for r in range(rounds) for n in range(NT)]:
                    for (w, a_h, a_l, o, start, stop) in terms(t):
                        wh, wl = w_hi[:, s, w * 512:(w + 1) * 512], w_lo[:, s, w * 512:(w + 1) * 512]
                        MM(o, a_h, wh, start=start, stop=False)
                        MM(o, a_l, wh, start=False, stop=False)
                        mm = MM(o, a_h, wl, start=False, stop=stop)
                    if last is not None and t < NT - 1:
                        mm.then_inc(last, 1)
                mm.then_inc(unit_done, 1)

            def turn_x2(c):
                pe.wait_ge(x2_ready, 4 * c + 4)
                pe.wait_ge(p_lo_done, PT)
                for f in range(4):
                    for t in range(NT):
                        mm = nc.tensor.transpose(ax_ps[:, 1 + f, t * P:(t + 1) * P], x2g[:, t, f * P:(f + 1) * P], ident[:, :])
                    mm.then_inc(x2_turned, 1)

            def out_group(c, is_first=False):
                us = Units(U_OUT, 6, c)
                for i, kn in enumerate(OUT_KT):
                    k0 = sum(OUT_KT[:i])
                    if i == 0 and is_first:
                        pe.wait_ge(gate_ready, 2 * KT)
                        pe.wait_ge(y_part, 2 * (KT - 1))

                    def terms(t):
                        if i == 0 and not is_first:
                            pe.wait_ge(x2_ready, 4 * c + (t - 3))
                        for k in range(kn):
                            if is_first and t == 0:
                                pe.wait_ge(a_lo_done, k0 + k + 1)
                            a = (k0 + k, slice(t * P, (t + 1) * P))
                            yield k, act_hi[:, a[0], a[1]], act_lo[:, a[0], a[1]], acc(t), k0 + k == 0, k0 + k == KT - 1

                    rows(us, i, terms, acc_done if i == 5 else None)
                    if i == 2 and is_first:
                        pe.wait_ge(p_landed, 16)
                        pe.wait_ge(y_part, 2 * KT)
                        for k in range(PT):
                            for t in range(NT):
                                mm = nc.tensor.transpose(ax_ps[:, 1 + k, t * P:(t + 1) * P], p_in[:, t, k * P:(k + 1) * P], ident[:, :])
                            mm.then_inc(p_turned, 1)
                    if i == 0 and not is_first:
                        turn_x2(c - 1)

            out_group(0, is_first=True)
            with pe.Fori(1, 4) as c:
                out_group(c)

            def ple_group(c, is_first=False):
                us = Units(U_PLE, 6, c)
                for i in range(6):
                    def terms(n):
                        t = n % NT
                        tok = slice(t * P, (t + 1) * P)
                        if i == 0 and n < NT:
                            if not is_first:
                                pe.wait_ge(pw_ready, 4 * c + (t - 3))
                            for k in range(PT):
                                yield k, p_hi[:, k, tok], p_lo[:, k, tok], ax_ps[:, 1 + t, :], k == 0, k == PT - 1
                            return
                        if i == 0:
                            if is_first:
                                pe.wait_ge(x2_ready, 13 + t)
                            else:
                                pe.wait_ge(g_ready, 4 * c + (t - 3))
                        for k in ([0] if i == 0 else range(3 * i - 2, 3 * i + 1)):
                            if is_first and t == 0:
                                pe.wait_ge(a_lo_done, KT + k + 1)
                            w = PT if i == 0 else k - (3 * i - 2)
                            yield w, act_hi[:, k, tok], act_lo[:, k, tok], acc(t), k == 0, k == KT - 1

                    rows(us, i, terms, acc_done if i == 5 else None, rounds=2 if i == 0 else 1)
                    if is_first and i == 1:
                        pe.wait_ge(pw_ready, 4)
                        turn_x2(3)

            ple_group(0, is_first=True)
            with pe.Fori(1, 4) as c:
                ple_group(c)


INPUTS = ["x", "p", "norm_g", "w_in", "hgrn_lb", "hgrn_onorm", "na_qnorm", "na_knorm", "na_rpb",
          "w_branch_a", "w_branch_b", "w_out", "ple_norm", "w_ple_gate", "w_ple"]


def kernel(**inputs):
    import numpy as np
    import concourse.bacc as bacc
    from concourse.bass_utils import run_bass_kernel_spmd

    nc = bacc.Bacc("TRN2", target_bir_lowering=False, num_devices=1)
    arrays, args = {}, []
    for name in INPUTS:
        a = np.ascontiguousarray(inputs[name])
        arrays[f"in_{name}"] = a
        args.append(nc.dram_tensor(f"in_{name}", a.shape, mybir.dt.from_np(a.dtype), kind="ExternalInput").ap())
    shape = np.asarray(inputs["x"]).shape
    args.append(nc.dram_tensor("out_0", shape, F32, kind="ExternalOutput").ap())
    build_kernel(nc, *args)
    r = run_bass_kernel_spmd(nc, [arrays], core_ids=[0])
    return r.results[0]["out_0"]
```
